# Optimizing a Trainium2 kernel written in Bass

```python
import jax, jax.numpy as jnp
from jax import lax
import numpy as np

D_MODEL = 2048
BATCH = 1
SEQ = 256
DEPTH = 2

EPS = 1e-6
NEG = -1e30
QB = 128

MLA_HEADS = 8
MLA_Q_RANK = 384
MLA_KV_RANK = 128
MLA_NOPE = 64
MLA_ROPE = 32
MLA_V = 64
MLA_QK = MLA_NOPE + MLA_ROPE
ROPE_THETA = 10000.0

DIL_HEADS = 12
DIL_HD = 64
DIL_W = DIL_HEADS * DIL_HD
DIL_PATTERNS = ((128, 1), (512, 4), (2048, 16))
N_BUCKETS = 32
BUCKET_MAX_DIST = 1024

ML_HEADS = 4
ML_HD = 192
ML_W = ML_HEADS * ML_HD
ML_CONV = 5
ML_CHUNK = 128
ML_F_BIAS_LO = 3.0
ML_F_BIAS_HI = 6.0

N_GROUPS = 4
EXPERTS_PER_GROUP = 4
N_EXPERTS = N_GROUPS * EXPERTS_PER_GROUP
MOE_TOPK = 2
D_EXPERT = 512

IN_SIZES = (MLA_Q_RANK, MLA_KV_RANK, MLA_ROPE, DIL_W, DIL_W, DIL_W, ML_W, ML_W, ML_W, 4 * ML_HEADS)
C_IN = sum(IN_SIZES)
D_MIX = MLA_HEADS * MLA_V + DIL_W + ML_W

kernel_name = 'hybrid_mla_dilated_mlstm_hmoe_encoder'

def rms_norm(x, g):
    xf = x.astype(jnp.float32)
    y = xf * lax.rsqrt(jnp.mean(xf * xf, axis=-1, keepdims=True) + EPS)
    return (y * g.astype(jnp.float32)).astype(x.dtype)

def rope_cos_sin(positions):
    half = MLA_ROPE // 2
    inv_freq = ROPE_THETA ** (-jnp.arange(half, dtype=jnp.float32) / half)
    ang = positions.astype(jnp.float32)[..., None] * inv_freq
    return jnp.cos(ang), jnp.sin(ang)

def apply_rope(x, cos, sin):
    xf = x.astype(jnp.float32)
    x1, x2 = jnp.split(xf, 2, axis=-1)
    return jnp.concatenate([x1 * cos - x2 * sin, x1 * sin + x2 * cos], axis=-1).astype(x.dtype)

def blocks_to_seq(out):
    nb, B, H, L, d = out.shape
    return out.transpose(1, 0, 3, 2, 4).reshape(B, nb * L, H * d)

def dense_block_attention(q, k, v):
    S = q.shape[2]
    scale = q.shape[-1] ** -0.5

    def one_block(start):
        qb = lax.dynamic_slice_in_dim(q, start, QB, axis=2)
        s = jnp.einsum('bhqd,bhkd->bhqk', qb, k, preferred_element_type=jnp.float32) * scale
        p = jax.nn.softmax(s, axis=-1)
        return jnp.einsum('bhqk,bhkd->bhqd', p.astype(v.dtype), v)

    return blocks_to_seq(lax.map(one_block, jnp.arange(S // QB, dtype=jnp.int32) * QB))

def mla_mixer(c_q, c_kv, k_rope, cos, sin, g_cq, w_uq, g_ckv, w_ukv, g_q, g_k):
    B, S, _ = c_q.shape
    q = (rms_norm(c_q, g_cq) @ w_uq).reshape(B, S, MLA_HEADS, MLA_QK)
    kv = (rms_norm(c_kv, g_ckv) @ w_ukv).reshape(B, S, MLA_HEADS, MLA_NOPE + MLA_V)
    q_rot = apply_rope(q[..., MLA_NOPE:], cos[:, :, None], sin[:, :, None])
    k_rot = apply_rope(k_rope, cos, sin)
    q = jnp.concatenate([q[..., :MLA_NOPE], q_rot], axis=-1)
    k = jnp.concatenate([kv[..., :MLA_NOPE],
                         jnp.broadcast_to(k_rot[:, :, None, :], (B, S, MLA_HEADS, MLA_ROPE))], axis=-1)
    v = kv[..., MLA_NOPE:]
    q = rms_norm(q, g_q).transpose(0, 2, 1, 3)
    k = rms_norm(k, g_k).transpose(0, 2, 1, 3)
    return dense_block_attention(q, k, v.transpose(0, 2, 1, 3))

def dilation_offsets():
    offs = []
    for w, d in DIL_PATTERNS:
        r = w // (2 * d)
        offs.append(np.arange(-r, r + 1) * d)
    return np.stack(offs)

def t5_buckets(rel):
    half = N_BUCKETS // 2
    max_exact = half // 2
    n = np.abs(rel)
    large = max_exact + (np.log(np.maximum(n, 1) / max_exact) / np.log(BUCKET_MAX_DIST / max_exact)
                         * (half - max_exact)).astype(np.int32)
    large = np.minimum(large, half - 1)
    return (rel > 0).astype(np.int32) * half + np.where(n < max_exact, n, large).astype(np.int32)

def dilated_mixer(q, k, v, rel_bias, g_q, g_k):
    B, S, _ = q.shape
    q = rms_norm(q.reshape(B, S, DIL_HEADS, DIL_HD), g_q).transpose(0, 2, 1, 3)
    k = rms_norm(k.reshape(B, S, DIL_HEADS, DIL_HD), g_k).transpose(0, 2, 1, 3)
    v = v.reshape(B, S, DIL_HEADS, DIL_HD).transpose(0, 2, 1, 3)
    offs = dilation_offsets()
    P, K = offs.shape
    flat = jnp.asarray(offs.reshape(-1), jnp.int32)
    bias = rel_bias.astype(jnp.float32)[jnp.asarray(t5_buckets(offs.reshape(-1)))].T
    scale = DIL_HD ** -0.5

    def one_block(start):
        qb = lax.dynamic_slice_in_dim(q, start, QB, axis=2)
        idx = start + jnp.arange(QB, dtype=jnp.int32)[:, None] + flat[None, :]
        valid = (idx >= 0) & (idx < S)
        idx = jnp.clip(idx, 0, S - 1)
        kg = k[:, :, idx]
        vg = v[:, :, idx].reshape(B, DIL_HEADS, QB, P, K, DIL_HD).astype(jnp.float32)
        s = jnp.einsum('bhqd,bhqkd->bhqk', qb, kg, preferred_element_type=jnp.float32) * scale
        s = jnp.where(valid[None, None], s + bias[None, :, None, :], NEG).reshape(B, DIL_HEADS, QB, P, K)
        m = jnp.max(s, axis=-1)
        p = jnp.exp(s - m[..., None])
        den = jnp.sum(p, axis=-1)
        o = jnp.einsum('bhqpk,bhqpkd->bhqpd', p, vg) / den[..., None]
        alpha = jax.nn.softmax(jnp.log(den) + m, axis=-1)
        return jnp.einsum('bhqp,bhqpd->bhqd', alpha, o).astype(v.dtype)

    return blocks_to_seq(lax.map(one_block, jnp.arange(S // QB, dtype=jnp.int32) * QB))

def mlstm_scan(q, k, v, log_i, log_f):
    B, H, S, d = q.shape
    L = ML_CHUNK
    nc = S // L

    def to_chunks(a):
        return jnp.moveaxis(a.reshape(B, H, nc, L, *a.shape[3:]), 2, 0)

    xs = (to_chunks(q), to_chunks(k), to_chunks(v), to_chunks(log_i), to_chunks(log_f))
    tril = jnp.tril(jnp.ones((L, L), dtype=bool))

    def step(carry, inp):
        C, n, m_prev = carry
        qc, kc, vc, li, lf = inp
        b = jnp.cumsum(lf, axis=-1)
        logw = jnp.where(tril, b[..., :, None] - b[..., None, :] + li[..., None, :], NEG)
        inter = b + m_prev[..., None]
        m = jnp.maximum(jnp.max(logw, axis=-1), inter)
        a = jnp.exp(logw - m[..., None]) * jnp.einsum('bhtd,bhsd->bhts', qc, kc)
        decay = jnp.exp(inter - m)
        num = jnp.einsum('bhts,bhsv->bhtv', a, vc) + decay[..., None] * jnp.einsum('bhtd,bhdv->bhtv', qc, C)
        den = jnp.sum(a, axis=-1) + decay * jnp.einsum('bhtd,bhd->bht', qc, n)
        h = num / jnp.maximum(jnp.abs(den), jnp.exp(-m))[..., None]
        m_new = m[..., -1]
        g = jnp.exp(b[..., -1:] - b + li - m_new[..., None])
        cd = jnp.exp(b[..., -1] + m_prev - m_new)
        C = cd[..., None, None] * C + jnp.einsum('bhs,bhsd,bhsv->bhdv', g, kc, vc)
        n = cd[..., None] * n + jnp.einsum('bhs,bhsd->bhd', g, kc)
        return (C, n, m_new), h

    init = (jnp.zeros((B, H, d, d), jnp.float32), jnp.zeros((B, H, d), jnp.float32),
            jnp.zeros((B, H), jnp.float32))
    _, hs = lax.scan(step, init, xs)
    return jnp.moveaxis(hs, 0, 2).reshape(B, H, S, d)

def mlstm_mixer(u, v, o_pre, gate_pre, conv_w, conv_b, w_q, w_k, gate_bias, g_out):
    B, S, _ = u.shape
    f32 = jnp.float32
    uc = lax.conv_general_dilated(u, conv_w[:, None, :].astype(u.dtype), window_strides=(1,),
                                  padding=((ML_CONV // 2, ML_CONV // 2),),
                                  dimension_numbers=('NWC', 'WIO', 'NWC'), feature_group_count=ML_W)
    uc = jax.nn.silu(uc + conv_b).reshape(B, S, ML_HEADS, ML_HD)
    q = jnp.einsum('bshd,hde->bhse', uc, w_q).astype(f32)
    k = jnp.einsum('bshd,hde->bhse', uc, w_k).astype(f32) * (ML_HD ** -0.5)
    vv = v.reshape(B, S, ML_HEADS, ML_HD).transpose(0, 2, 1, 3).astype(f32)
    pre = gate_pre.astype(f32).reshape(B, S, 2, 2, ML_HEADS) + gate_bias.astype(f32)
    log_i = jnp.transpose(pre[:, :, :, 0], (2, 0, 3, 1))
    log_f = jnp.transpose(jax.nn.log_sigmoid(pre[:, :, :, 1]), (2, 0, 3, 1))
    h_fwd = mlstm_scan(q, k, vv, log_i[0], log_f[0])
    rev = lambda a: jnp.flip(a, axis=2)
    h_bwd = rev(mlstm_scan(rev(q), rev(k), rev(vv), rev(log_i[1]), rev(log_f[1])))
    h = (h_fwd + h_bwd).transpose(0, 2, 1, 3)
    h = rms_norm(h, g_out.reshape(ML_HEADS, ML_HD)) * jax.nn.sigmoid(o_pre.astype(f32)).reshape(B, S, ML_HEADS, ML_HD)
    return h.reshape(B, S, ML_W).astype(u.dtype)

def hier_moe(x, wg, bg, we, be, w_gate, w_up, w_down):
    B, S, _ = x.shape
    f32 = jnp.float32
    g_logits = (x @ wg).astype(f32) + bg.astype(f32)
    grp = jnp.argmax(g_logits, axis=-1)
    p_grp = jnp.max(jax.nn.softmax(g_logits, axis=-1), axis=-1)
    e_logits = ((x @ we).astype(f32) + be.astype(f32)).reshape(B, S, N_GROUPS, EXPERTS_PER_GROUP)
    e_sel = jnp.take_along_axis(e_logits, grp[..., None, None], axis=2)[..., 0, :]
    top_v, top_i = lax.top_k(e_sel, MOE_TOPK)
    w = jax.nn.softmax(top_v, axis=-1) * p_grp[..., None]
    eid = grp[..., None] * EXPERTS_PER_GROUP + top_i
    comb = jnp.sum(jax.nn.one_hot(eid, N_EXPERTS, dtype=f32) * w[..., None], axis=-2)
    h = jax.nn.silu(jnp.einsum('bsd,edf->bsef', x, w_gate)) * jnp.einsum('bsd,edf->bsef', x, w_up)
    h = h * comb[..., None].astype(h.dtype)
    return jnp.einsum('bsef,efd->bsd', h, w_down)

def setup_inputs(seed: int = 0) -> dict:
    key = jax.random.key(seed)
    ks = jax.random.split(key, 32)
    f32 = jnp.float32
    L = DEPTH

    def nrm(k, shape, scale):
        return jax.random.normal(k, shape, f32) * scale

    def gain(k, shape):
        return 1.0 + 0.05 * jax.random.normal(k, shape, f32)

    i_bias = nrm(ks[16], (L, 2, 1, ML_HEADS), 0.1)
    f_bias = jnp.linspace(ML_F_BIAS_LO, ML_F_BIAS_HI, ML_HEADS, dtype=f32) + nrm(ks[17], (L, 2, 1, ML_HEADS), 0.1)
    return {
        'x': nrm(ks[0], (BATCH, SEQ, D_MODEL), 1.0),
        'positions': jnp.arange(SEQ, dtype=jnp.int32)[None, :]
                     + jax.random.randint(ks[1], (BATCH, 1), 0, 4096, dtype=jnp.int32),
        'rel_bias': nrm(ks[2], (N_BUCKETS, DIL_HEADS), 0.2),
        'norm_mix': gain(ks[3], (L, D_MODEL)),
        'w_in': nrm(ks[4], (L, D_MODEL, C_IN), D_MODEL ** -0.5),
        'mla_norm_cq': gain(ks[5], (L, MLA_Q_RANK)),
        'mla_w_uq': nrm(ks[6], (L, MLA_Q_RANK, MLA_HEADS * MLA_QK), MLA_Q_RANK ** -0.5),
        'mla_norm_ckv': gain(ks[7], (L, MLA_KV_RANK)),
        'mla_w_ukv': nrm(ks[8], (L, MLA_KV_RANK, MLA_HEADS * (MLA_NOPE + MLA_V)), MLA_KV_RANK ** -0.5),
        'mla_q_norm': gain(ks[9], (L, MLA_QK)),
        'mla_k_norm': gain(ks[10], (L, MLA_QK)),
        'dil_q_norm': gain(ks[11], (L, DIL_HD)),
        'dil_k_norm': gain(ks[12], (L, DIL_HD)),
        'ml_conv_w': nrm(ks[13], (L, ML_CONV, ML_W), ML_CONV ** -0.5),
        'ml_conv_b': nrm(ks[14], (L, ML_W), 0.02),
        'ml_w_q': nrm(ks[15], (L, ML_HEADS, ML_HD, ML_HD), ML_HD ** -0.5),
        'ml_w_k': nrm(ks[18], (L, ML_HEADS, ML_HD, ML_HD), ML_HD ** -0.5),
        'ml_gate_bias': jnp.concatenate([i_bias, f_bias], axis=2),
        'ml_out_norm': gain(ks[19], (L, ML_W)),
        'w_out': nrm(ks[20], (L, D_MIX, D_MODEL), D_MIX ** -0.5),
        'norm_ffn': gain(ks[21], (L, D_MODEL)),
        'router_group_w': nrm(ks[22], (L, D_MODEL, N_GROUPS), D_MODEL ** -0.5),
        'router_group_b': nrm(ks[23], (L, N_GROUPS), 0.01),
        'router_expert_w': nrm(ks[24], (L, D_MODEL, N_EXPERTS), D_MODEL ** -0.5),
        'router_expert_b': nrm(ks[25], (L, N_EXPERTS), 0.01),
        'moe_w_gate': nrm(ks[26], (L, N_EXPERTS, D_MODEL, D_EXPERT), D_MODEL ** -0.5),
        'moe_w_up': nrm(ks[27], (L, N_EXPERTS, D_MODEL, D_EXPERT), D_MODEL ** -0.5),
        'moe_w_down': nrm(ks[28], (L, N_EXPERTS, D_EXPERT, D_MODEL), D_EXPERT ** -0.5),
    }

def reference(x, positions, rel_bias, norm_mix, w_in, mla_norm_cq, mla_w_uq, mla_norm_ckv, mla_w_ukv,
              mla_q_norm, mla_k_norm, dil_q_norm, dil_k_norm, ml_conv_w, ml_conv_b, ml_w_q, ml_w_k,
              ml_gate_bias, ml_out_norm, w_out, norm_ffn, router_group_w, router_group_b,
              router_expert_w, router_expert_b, moe_w_gate, moe_w_up, moe_w_down):
    cos, sin = rope_cos_sin(positions)
    split_at = np.cumsum(IN_SIZES)[:-1].tolist()
    for l in range(DEPTH):
        xn = rms_norm(x, norm_mix[l])
        c_q, c_kv, k_rope, dq, dk, dv, mu, mv, mo, mg = jnp.split(xn @ w_in[l], split_at, axis=-1)
        y_mla = mla_mixer(c_q, c_kv, k_rope, cos, sin, mla_norm_cq[l], mla_w_uq[l], mla_norm_ckv[l],
                          mla_w_ukv[l], mla_q_norm[l], mla_k_norm[l])
        y_dil = dilated_mixer(dq, dk, dv, rel_bias, dil_q_norm[l], dil_k_norm[l])
        y_ml = mlstm_mixer(mu, mv, mo, mg, ml_conv_w[l], ml_conv_b[l], ml_w_q[l], ml_w_k[l],
                           ml_gate_bias[l], ml_out_norm[l])
        x = x + jnp.concatenate([y_mla, y_dil, y_ml], axis=-1) @ w_out[l]
        x = x + hier_moe(rms_norm(x, norm_ffn[l]), router_group_w[l], router_group_b[l],
                         router_expert_w[l], router_expert_b[l], moe_w_gate[l], moe_w_up[l], moe_w_down[l])
    return x


_drawn_inputs = setup_inputs


def setup_inputs(seed=0):
    import zlib

    import numpy as np

    out = dict(_drawn_inputs(seed))
    spreads = {}
    factors = {'mla_norm_cq': 4.76, 'mla_q_norm': 5.674, 'mla_k_norm': 3.303, 'dil_k_norm': 3.426}
    for name, (base, spread) in spreads.items():
        noise = np.random.default_rng([zlib.crc32(name.encode()), seed]).standard_normal(out[name].shape)
        drawn = base * np.exp(spread * noise) if base else spread * noise
        out[name] = __import__('jax').numpy.asarray(drawn.astype(out[name].dtype))
    for name, factor in factors.items():
        out[name] = (out[name] * factor).astype(out[name].dtype)
    return out
```

```python
from contextlib import ExitStack

import numpy as np

import concourse.bass as bass
from concourse import mybir

F32 = mybir.dt.float32
I32 = mybir.dt.int32
ALU = mybir.AluOpType
ACT = mybir.ActivationFunctionType
AX = mybir.AxisListType.X

P = 128
S = 256
NT = S // P
D = 2048
KT = D // P
DEPTH = 2
EPS = 1e-6
NEG = -1e30

H_A, QR, KVR, NOPE, ROPE, DV_A = 8, 384, 128, 64, 32, 64
QK_A = NOPE + ROPE
HALF = ROPE // 2
ROPE_THETA = 10000.0
H_D, HD_D = 12, 64
W_D = H_D * HD_D
PATTERNS = ((128, 1), (512, 4), (2048, 16))
N_BUCKETS, BUCKET_MAX = 32, 1024
H_M, HD_M, TAPS = 4, 192, 5
W_M = H_M * HD_M
CB = HD_M // 2
NCB = W_M // CB
NG, EPG, F_E = 4, 4, 512
NE = NG * EPG

C_IN = QR + KVR + ROPE + 3 * W_D + 3 * W_M + 4 * H_M
D_DQ = QR + KVR + ROPE
CQ, CKV = 0, QR
KR = QR + KVR
MG = KR + ROPE
DQ = MG + 4 * H_M
DK, DV = DQ + W_D, DQ + 2 * W_D
MU = DQ + 3 * W_D
MV, MO = MU + W_M, MU + 2 * W_M
CH = 256
SLOT = KT * CH
NSLOT = 6
N_MAIN = (C_IN - D_DQ - 4 * H_M) // CH
MAIN_ITERS = N_MAIN // NSLOT
N_OUT = D // CH

R_MIX, R_FFN = 0, KT
R_CQ = 2 * KT
R_CKV = R_CQ + QR // P
R_MLO = R_CKV + 1
R_DQ = R_MLO + W_M // P
R_DK = R_DQ + 1
N_ROW = R_DK + 1
R_CW, R_CB = 0, TAPS * NCB
R_AQ = R_CB + NCB
R_AK = R_AQ + 1
N_ROW96 = R_AK + 1
K_ID, K_FLIP, K_MASK = 0, P, 2 * P
K_FREQ = 3 * P
K_KEYG = K_FREQ + HALF
K_KEYE = K_KEYG + NG
N_CONST = K_KEYE + NE


def t5_buckets(rel):
    half = N_BUCKETS // 2
    exact = half // 2
    n = np.abs(rel)
    large = exact + (np.log(np.maximum(n, 1) / exact) / np.log(BUCKET_MAX / exact) * (half - exact)).astype(np.int32)
    large = np.minimum(large, half - 1)
    return (rel > 0).astype(np.int32) * half + np.where(n < exact, n, large).astype(np.int32)


def shape_constants():
    c = np.zeros((P, N_CONST), np.float32)
    c[:, K_ID:K_ID + P] = np.eye(P)
    c[:, K_FLIP:K_FLIP + P] = np.eye(P)[::-1]
    s, t = np.arange(P)[:, None], np.arange(P)[None, :]
    c[:, K_MASK:K_MASK + P] = np.where(s <= t, 0.0, NEG)
    c[:, K_FREQ:K_FREQ + HALF] = np.float32(ROPE_THETA) ** (-np.arange(HALF, dtype=np.float32) / np.float32(HALF))
    c[:, K_KEYG:K_KEYG + NG] = np.arange(NG, 0, -1)
    c[:, K_KEYE:K_KEYE + NE] = np.arange(NE, 0, -1)
    off = np.arange(2 * S) - (S - 1)
    onehot = np.zeros((N_BUCKETS, 2 * S), np.float32)
    onehot[t5_buckets(off), np.arange(2 * S)] = 1.0
    count = sum(((np.abs(off) <= w // 2) & (off % d == 0)).astype(np.int32) for w, d in PATTERNS)
    count[-1] = 0
    lncount = np.where(count > 0, np.log(np.maximum(count, 1)), NEG).astype(np.float32)
    return c, onehot, np.broadcast_to(lncount, (H_D, 2 * S)).copy()


class Uses:

    def __init__(self, n):
        self.n, self.at = n, {}
        self.count = {"pre": [0] * n, "layer": [0] * n, "post": [0] * n}
        self.part = "pre"

    def once(self, name, r):
        c = self.count[self.part]
        self.at[name] = (self.part, r, c[r], 0)
        c[r] += 1

    def loop(self, names, iters):
        c = self.count[self.part]
        per = [sum(r == q for _, r in names) for q in range(self.n)]
        seen = [0] * self.n
        for name, r in names:
            self.at[name] = (self.part, r, c[r] + seen[r], per[r])
            seen[r] += 1
        for q in range(self.n):
            c[q] += iters * per[q]

    def where(self, name):
        return self.at[name][1]

    def before(self, name, l=0, i=0):
        part, r, k, stride = self.at[name]
        if part == "pre":
            return k
        k += self.count["pre"][r]
        if part == "post":
            return k + DEPTH * self.count["layer"][r]
        return l * self.count["layer"][r] + k + (i * stride if stride else 0)


def plan_banks():
    b = Uses(8)
    for j in range(NT * KT // 4):
        b.once(f"x{j}", j % 8)
    for l in range(DEPTH):
        b.once(f"par{l}", 2 * l)
        b.once(f"par96{l}", 2 * l + 1)
    b.once("bias", 4)
    b.part = "layer"
    b.once("ssq", 0)
    for j in range(3):
        b.once(f"c{j}", 1 + j)
    for t in range(NT):
        b.once(f"lat{t}", 4 + t)
    for t in range(NT):
        for j in range(4):
            b.once(f"up{t}{j}", [6, 7, 0, 1, 2, 3, 4, 5][4 * t + j])
    b.loop([(f"m{j}", j) for j in range(NSLOT)], MAIN_ITERS - 1)
    plan_attention(b, "a", H_A, 1)
    for j in range(NSLOT):
        b.once(f"z{j}", j)
    plan_attention(b, "d", H_D, 2)
    for d in range(2):
        b.once(f"rows{d}", d)
    for m in range(NCB // 2):
        b.once(f"mu{m}", 2 + m)
    b.once("gcols", 6)
    for h in range(H_M + 1):
        if h < H_M:
            b.once(f"mq{h}", 0)
            b.once(f"mk{h}", 1)
            b.once(f"w{h}0", 2)
            b.once(f"w{h}1", 3)
            b.once(f"ms{h}", 4 + h % 2)
        if h >= 1:
            b.once(f"n{h - 1}0", 6)
            b.once(f"n{h - 1}1", 7)
    for j in range(KT // 2):
        b.once(f"y{j}", j)
    for j in range(N_OUT):
        b.once(f"o{j}", j)
    b.once("ssq2", 0)
    b.once("route", 1)
    b.once("combT", 2)
    for j in range(NE // 2):
        b.once(f"cb{j}", j)
    b.loop([("g0", 0), ("u0", 1), ("g1", 2), ("u1", 3)] + [(f"dn{j}", 4 + j % 4) for j in range(KT // 2)], NE)
    b.part = "post"
    for j in range(NT * KT // 4):
        b.once(f"f{j}", j % 8)
    return b


def plan_attention(b, k, heads, per):
    for s in range(heads + 3):
        if s < heads and s % per == 0:
            b.once(f"{k}t{s // per}", s // per % 2)
        if 1 <= s <= heads:
            b.once(f"{k}s{s - 1}", 2 + (s - 1) % 2)
        if 2 <= s <= heads + 1:
            b.once(f"{k}p{s - 2}", 4 + s % 2)
        if s >= 3:
            b.once(f"{k}o{s - 3}", 6 + (s - 3) % 2)


ONCE = [(f"c{j}", 1) for j in range(3)] + [("up", 1)]
MAIN = [(f"m{j}", MAIN_ITERS - 1) for j in range(NSLOT)]
THEN = [(f"z{j}", 1) for j in range(NSLOT)] + [("mw", 1)] + [(f"o{j}", 1) for j in range(N_OUT)]
EXPERT = [(n, NE) for n in ("g0", "u0", "g1", "u1", "d0", "d1")]


def plan_slots():
    r = Uses(NSLOT)
    r.part = "layer"
    at = 0
    for group in (ONCE, MAIN, THEN, EXPERT):
        names = []
        for name, iters in group:
            names.append((name, at % NSLOT))
            at += 1
        if group in (MAIN, EXPERT):
            r.loop(names, group[0][1])
        else:
            for name, s in names:
                r.once(name, s)
    return r


BANKS, SLOTS = plan_banks(), plan_slots()
LAST_READER = {"up": "up13", "mw": f"mk{H_M - 1}", "d0": "dn3", "d1": "dn7"}


DVE_PRE, DVE_LAYER, ACT_LAYER = 17, 136, 20


class Steps:

    def __init__(self, eng, sem, pre, per_layer):
        self.eng, self.sem, self.pre, self.per_layer = eng, sem, pre, per_layer
        self.n, self.l, self.base = 0, None, 0

    def did(self, ins):
        ins.then_inc(self.sem, 1)
        self.n += 1

    def wait(self):
        self.eng.wait_ge(self.sem, self.n if self.l is None else self.base + self.n)

    def enter_layer(self, l):
        assert self.n == self.pre, f"pre {self.n}"
        self.l, self.n = l, 0
        self.base = l * self.per_layer + self.pre

    def enter_loop(self, i, per_turn):
        self.kept = (self.n, self.base, per_turn)
        self.base = self.base + self.n + i * per_turn
        self.n = 0

    def leave_loop(self, turns):
        n, base, per_turn = self.kept
        assert self.n == per_turn, f"turn {self.n}"
        self.n, self.base = n + turns * per_turn, base

    def leave_layer(self):
        assert self.n == self.per_layer, f"layer {self.n}"
        self.n, self.l = self.pre + DEPTH * self.per_layer, None


def build(nc, a, consts, onehot, lncount, out):
    with ExitStack() as ctx:
        def sb(name, shape, dt=F32):
            return ctx.enter_context(nc.sbuf_tensor(name, shape, dt))

        def sem(name):
            return ctx.enter_context(nc.semaphore(name))

        ring = sb("ring", [P, NSLOT, SLOT])
        X = sb("X", [P, KT, S])
        XN = sb("XN", [P, KT, S])
        PR = sb("PR", [P, NT, C_IN])
        BIAS = sb("BIAS", [P, H_D, S + P])
        K = sb("K", [P, N_CONST])
        scr = sb("scr", [P, 3 * 1024])
        v_mla = sb("v_mla", [P, NT, H_A * DV_A])
        ones = sb("ones", [P, P])
        par = sb("par", [P, DEPTH, N_ROW])
        par96 = sb("par96", [CB, DEPTH, N_ROW96])
        col, col96 = sb("col", [P, N_ROW]), sb("col96", [CB, N_ROW96])
        brow = sb("brow", [P, DEPTH, 4 * H_M + NG + NE])
        cs = sb("cs", [P, 2, NT, HALF])
        pos_i = sb("pos_i", [P, NT], I32)
        pos_f = sb("pos_f", [P, NT])
        eps = sb("eps", [P, 1])
        std_x, rstd_x = sb("std_x", [P, NT]), sb("rstd_x", [P, NT])
        ss_lat, std_lat, rstd_lat = (sb(n, [P, 2, NT]) for n in ("ss_lat", "std_lat", "rstd_lat"))
        ss_a, rstd_a = sb("ss_a", [P, 2, NT, H_A]), sb("rstd_a", [P, 2, NT, H_A])
        ss_d, rstd_d = sb("ss_d", [P, 2, NT, H_D]), sb("rstd_d", [P, 2, NT, H_D])
        mx, nmx, psum_p = (sb(n, [P, 2, NT]) for n in ("mx", "nmx", "psum_p"))
        rs = sb("rs", [P, 4, NT])
        gcol = sb("gcol", [P, 2, 2, NT, H_M])
        std_d = sb("std_d", [P, 2, NT, H_D])
        std_a = sb("std_a", [P, 2, NT, H_A])
        std_m = sb("std_m", [P, H_M, NT])
        em = sb("em", [P, 2, NT, H_M])
        dn = sb("dn", [P, 2, 2, NT])
        ss_m, rstd_m = sb("ss_m", [P, H_M, NT]), sb("rstd_m", [P, H_M, NT])
        ps = ctx.enter_context(nc.psum_tensor("ps", [P, 8, 512], F32))
        bias_dram = nc.dram_tensor("bias_dram", (H_D, 2 * S), F32).ap()

        ident, flip = K[:, K_ID:K_ID + P], K[:, K_FLIP:K_FLIP + P]
        mask = K[:, K_MASK:K_MASK + P]
        prf = PR[:, :, :].rearrange("p t c -> p (t c)")
        SQ = prf[:, 0:KT * S].rearrange("p (k s) -> p k s", k=KT)
        combB = prf[:, KT * S:2 * KT * S].rearrange("p (e s) -> p e s", e=NE)
        q_mla, k_mla = PR[:, :, MV:MV + W_M], PR[:, :, MO:MO + W_M]
        qkT = scr[:, 0:1024].rearrange("p (b n) -> p b n", b=2)
        prob = scr[:, 1024:2048].rearrange("p (b t n) -> p b t n", b=2, t=NT)
        pT = scr[:, 2048:3072].rearrange("p (b t n) -> p b t n", b=2, t=NT)
        latT = scr[:, 2048:3072].rearrange("p (k s) -> p k s", s=S)
        rtmp = scr[:, 1024:2048].rearrange("p (a t h n) -> p a t h n", a=4, t=NT, h=H_A)
        decay = scr[:, 0:4 * 3 * P].rearrange("p (b d n) -> p b d n", b=2, d=2)
        hT = scr[:, 0:4 * S].rearrange("p (k n) -> p k n", k=4)
        ang = scr[:, 0:4 * NT * HALF].rearrange("p (a t n) -> p a t n", a=4, t=NT)
        rt = scr[:, 1792:1792 + 6 * NT * NE].rearrange("p (a t n) -> p a t n", a=6, t=NT)
        lg = scr[:, 1984:1984 + NT * (NG + NE)].rearrange("p (t n) -> p t n", t=NT)
        rs1 = scr[:, 2024:2040].rearrange("p (a t) -> p a t", t=NT)
        w_rt = scr[:, 2048:2048 + KT * (NG + NE)].rearrange("p (k n) -> p k n", k=KT)
        combT = scr[0:NE, 1536:1536 + S]
        sg = scr[:, 2048:3072].rearrange("p (b n) -> p b n", b=2)
        xnf = XN[:, :, :].rearrange("p k s -> p (k s)")
        uc = xnf[0:CB, 0:NCB * S].rearrange("p (b s) -> p b s", b=NCB)
        mqk = xnf[0:CB, NCB * S:2 * NCB * S].rearrange("p (b q n) -> p b q n", b=2, q=2)
        raw = xnf[0:N_ROW, 0:DEPTH * P].rearrange("p (l n) -> p l n", l=DEPTH)
        raw96 = xnf[0:N_ROW96, 512:512 + DEPTH * CB].rearrange("p (l n) -> p l n", l=DEPTH)
        oh = xnf[0:N_BUCKETS, 1024:1024 + 2 * S]
        rb = xnf[0:N_BUCKETS, 1536:1536 + H_D]
        lnc = xnf[0:H_D, 2048:2048 + 2 * S]
        fbias = scr[0:H_D, 512:512 + 2 * S]

        def grow(d, j):
            return PR[0:H_M, d, DK + j * S:DK + (j + 1) * S]

        slot_full = [sem(f"slot_full{s}") for s in range(NSLOT)]
        psum_full = [sem(f"psum_full{b}") for b in range(8)]
        psum_free = [sem(f"psum_free{b}") for b in range(8)]
        dve_steps, act_steps = sem("dve_steps"), sem("act_steps")
        x_in, par_in, const_in, bias_in, bias_out, pos_in, rw_in, done = map(
            sem, ("x_in", "par_in", "const_in", "bias_in", "bias_out", "pos_in", "rw_in", "done"))
        c2_full, up_full, mw_full = sem("c2_full"), sem("up_full"), sem("mw_full")
        ones_set, ang_set = sem("ones_set"), sem("ang_set")

        stages = {}

        def stage(name, n=1):
            stages[name] = (sem(name), n)

        def signal(name):
            return stages[name][0], 1

        def after(name, l, j=0):
            s, n = stages[name]
            return s, l * n + (j + 1)

        for name, n in (("cols", 2), ("sq", 4), ("xg", KT), ("rstd_x", 1), ("lat_std", 1), ("lat_n", 1),
                        ("a_roped", 1), ("a_sq", 1), ("a_ss", 1), ("a_std", 1), ("a_n", 1),
                        ("d_sq", 1), ("d_ss", 1), ("d_std", 1), ("d_n", 1), ("nmax", H_A + H_D), ("rsum", H_A + H_D),
                        ("gate_b", 1), ("gate_ln", 2), ("rows_ready", 2), ("em_ready", 1), ("uc_ready", H_M),
                        ("r_ready", H_M), ("m_std", 1), ("y_ml", 1), ("sq2", 4), ("xn2", KT),
                        ("e_in", 2), ("e_exp", 2), ("comb", 1), ("h_gated", 2 * NE)):
            stage(name, n)

        def bank(name):
            return ps[:, BANKS.where(name), :]

        def ready(name, l=0, i=0):
            return psum_full[BANKS.where(name)], BANKS.before(name, l, i) + 1

        def freed(name, l=0, i=0):
            return psum_free[BANKS.where(name)], BANKS.before(name, l, i)

        def copied(name, l=0, i=0):
            return psum_free[BANKS.where(name)], BANKS.before(name, l, i) + 1

        def made(name):
            return psum_full[BANKS.where(name)], 1

        def read(name):
            return psum_free[BANKS.where(name)], 1

        def slot(name):
            return ring[:, SLOTS.where(name), :]

        def empty(name, l, turn=0):
            if not (isinstance(turn, int) and turn == 0):
                return ready(LAST_READER.get(name, name), l, turn - 1)
            s = SLOTS.where(name)
            order = [n for n, _ in ONCE + MAIN + THEN + EXPERT if SLOTS.where(n) == s]
            before = order[order.index(name) - 1]
            turns = dict(ONCE + MAIN + THEN + EXPERT)[before]
            earlier = order.index(name) == 0
            return ready(LAST_READER.get(before, before), l - 1 if earlier else l, turns - 1)

        skip = {}
        for n in ("c2", "up", "mw"):
            skip.setdefault(SLOTS.where(n), []).append(SLOTS.at[n][2])

        def loaded(name, l, i=0):
            s = SLOTS.where(name)
            k, stride = SLOTS.at[name][2:]
            own = skip.get(s, [])
            k -= sum(o < k for o in own)
            n = SLOTS.count["layer"][s] - len(own)
            return slot_full[s], 16 * (l * n + (k + 1) + (i * stride if stride else 0))

        def heads(t, off, n, w):
            return PR[:, t, off:off + n * w].rearrange("p (h w) -> p h w", h=n)

        block = ctx.enter_context(nc.Block())

        @block.sync
        def _(sp):
            for t in range(NT):
                sp.dma_start(PR[:, t, 0:D], a["x"][0, t * P:(t + 1) * P, :]).then_inc(x_in, 16)

            def w_cols(l, lo, n):
                return a["w_in"][l, :, lo:lo + n].rearrange("(k p) c -> p k c", p=P)

            def load(name, l, src, turn=0, k=KT):
                sp.wait_ge(*empty(name, l, turn))
                sp.dma_start(slot(name).rearrange("p (k c) -> p k c", k=k), src).then_inc(
                    slot_full[SLOTS.where(name)], 16)

            with sp.Fori(0, DEPTH) as l:
                for j in range(2):
                    load(f"c{j}", l, w_cols(l, j * CH, CH))
                sp.wait_ge(*empty("c2", l))
                nar = slot("c2")[:, 0:KT * 48].rearrange("p (k c) -> p k c", k=KT)
                sp.dma_start(nar[:, :, 0:ROPE], w_cols(l, KR, ROPE)).then_inc(c2_full, 16)
                sp.dma_start(nar[:, :, ROPE:48], w_cols(l, C_IN - 4 * H_M, 4 * H_M)).then_inc(c2_full, 16)
                sp.wait_ge(*empty("up", l))
                sp.dma_start(slot("up")[:, 0:3 * W_D].rearrange("p (k c) -> p k c", k=3),
                             a["mla_w_uq"][l].rearrange("(k p) c -> p k c", p=P)).then_inc(up_full, 16)
                sp.dma_start(slot("up")[:, 3 * W_D:3 * W_D + 1024], a["mla_w_ukv"][l]).then_inc(up_full, 16)
                for i in range(MAIN_ITERS - 1):
                    for j in range(NSLOT):
                        load(f"m{j}", l, w_cols(l, D_DQ + (i * NSLOT + j) * CH, CH), i)
                for j in range(NSLOT):
                    load(f"z{j}", l, w_cols(l, D_DQ + ((MAIN_ITERS - 1) * NSLOT + j) * CH, CH))
                sp.wait_ge(*empty("mw", l))
                for n, w in enumerate(("ml_w_q", "ml_w_k")):
                    sp.dma_start(slot("mw")[0:CB, n * NCB * HD_M:(n + 1) * NCB * HD_M].rearrange("p (b e) -> p b e", b=NCB),
                                 a[w][l].rearrange("h (b p) e -> p (h b) e", p=CB)).then_inc(mw_full, 16)
                for j in range(N_OUT):
                    load(f"o{j}", l, a["w_out"][l, :, j * CH:(j + 1) * CH].rearrange("(k p) c -> p k c", p=P))
                sp.wait_ge(*after("y_ml", l))
                sp.dma_start(w_rt[:, :, 0:NG], a["router_group_w"][l].rearrange("(k p) c -> p k c", p=P)).then_inc(rw_in, 16)
                sp.dma_start(w_rt[:, :, NG:], a["router_expert_w"][l].rearrange("(k p) c -> p k c", p=P)).then_inc(rw_in, 16)

                def load_expert(e):
                    for half in range(2):
                        for n, w in (("g", "moe_w_gate"), ("u", "moe_w_up")):
                            load(f"{n}{half}", l, a[w][l].rearrange("e (k p) f -> e p k f", p=P)
                                 [bass.ds(e, 1), :, :, half * CH:(half + 1) * CH].rearrange("e p k f -> (e p) k f"), e)
                    for half in range(2):
                        load(f"d{half}", l, a["moe_w_down"][l].rearrange("e (k p) c -> e p k c", p=P)
                             [bass.ds(e, 1), :, :, half * 1024:(half + 1) * 1024].rearrange("e p k c -> (e p) k c"), e, k=4)

                load_expert(0)
                with sp.Fori(1, NE) as e:
                    load_expert(e)
            for t in range(NT):
                for g in range(KT // 4):
                    sp.wait_ge(*copied(f"f{t * KT // 4 + g}"))
                sp.dma_start(out[0, t * P:(t + 1) * P, :], PR[:, t, 0:D]).then_inc(done, 16)
            sp.wait_ge(done, 16 * NT)

        @block.gpsimd
        def _(pool):
            pool.dma_start(K[:, :], consts).then_inc(const_in, 16)
            for l in range(DEPTH):
                r = raw[:, l, :]
                for at, n, src in ((R_MIX, KT, a["norm_mix"][l]), (R_FFN, KT, a["norm_ffn"][l]),
                                   (R_CQ, 3, a["mla_norm_cq"][l]), (R_CKV, 1, a["mla_norm_ckv"][l]),
                                   (R_MLO, 6, a["ml_out_norm"][l])):
                    pool.dma_start(r[at:at + n, :], src.rearrange("(r c) -> r c", c=P)).then_inc(par_in, 16)
                for at, src in ((R_DQ, a["dil_q_norm"][l]), (R_DK, a["dil_k_norm"][l])):
                    for h in range(2):
                        pool.dma_start(r[at:at + 1, h * HD_D:(h + 1) * HD_D], src.unsqueeze(0)).then_inc(par_in, 16)
                r = raw96[:, l, :]
                pool.dma_start(r[R_CW:R_CW + TAPS * NCB, :], a["ml_conv_w"][l].rearrange("t (b c) -> (t b) c", c=CB)).then_inc(par_in, 16)
                pool.dma_start(r[R_CB:R_CB + NCB, :], a["ml_conv_b"][l].rearrange("(b c) -> b c", c=CB)).then_inc(par_in, 16)
                pool.dma_start(r[R_AQ:R_AQ + 1, :], a["mla_q_norm"][l].unsqueeze(0)).then_inc(par_in, 16)
                pool.dma_start(r[R_AK:R_AK + 1, :], a["mla_k_norm"][l].unsqueeze(0)).then_inc(par_in, 16)
                for at, n, src in ((0, 4 * H_M, a["ml_gate_bias"][l].rearrange("d i h -> (d i h)")),
                                   (4 * H_M, NG, a["router_group_b"][l]), (4 * H_M + NG, NE, a["router_expert_b"][l])):
                    pool.dma_start(brow[:, l, at:at + n], src.partition_broadcast(P)).then_inc(par_in, 16)
            pool.dma_start(oh, onehot).then_inc(bias_in, 16)
            pool.dma_start(lnc, lncount).then_inc(bias_in, 16)
            pool.dma_start(rb, a["rel_bias"]).then_inc(bias_in, 16)
            pool.dma_start(pos_i[:, :], a["positions"][0].rearrange("(t p) -> p t", p=P),
                           allow_slow_non_contiguous=True).then_inc(pos_in, 16)
            pool.wait_ge(*copied("bias"))
            pool.dma_start(bias_dram, fbias).then_inc(bias_out, 16)
            pool.wait_ge(bias_out, 16)
            pool.dma_start(BIAS[:, :, :], bass.AP(bias_dram.tensor, 0, [[1, P], [2 * S, H_D], [1, S + P]])).then_inc(bias_out, 16)
            pool.wait_ge(bias_out, 32)

        N_PAR = DEPTH * 16 * (5 + 4 + 4 + 3)

        @block.tensor
        def _(pe):
            def mm(o, lhsT, rhs, start=True, stop=True):
                return pe.matmul(o, lhsT, rhs, start=start, stop=stop, skip_group_check=True)

            pe.wait_ge(const_in, 16)
            pe.wait_ge(ones_set, 2)
            for t in range(NT):
                pe.wait_ge(x_in, 16 * (t + 1))
                if t == 0:
                    pe.wait_ge(x_in, 16 * NT)
                for g in range(KT // 4):
                    name = f"x{t * KT // 4 + g}"
                    pe.wait_ge(*freed(name))
                    for q in range(4):
                        last = pe.transpose(bank(name)[:, q * P:(q + 1) * P], PR[:, t, (4 * g + q) * P:(4 * g + q + 1) * P], ident)
                    last.then_inc(*made(name))
            pe.wait_ge(par_in, N_PAR)
            for l in range(DEPTH):
                pe.wait_ge(*freed(f"par{l}"))
                pe.transpose(bank(f"par{l}")[:, 0:N_ROW], raw[:, l, :], K[0:N_ROW, K_ID:K_ID + N_ROW]).then_inc(*made(f"par{l}"))
                pe.wait_ge(*freed(f"par96{l}"))
                pe.transpose(bank(f"par96{l}")[0:CB, 0:N_ROW96], raw96[:, l, :], K[0:N_ROW96, K_ID:K_ID + N_ROW96]).then_inc(*made(f"par96{l}"))
            pe.wait_ge(bias_in, 48)
            pe.wait_ge(*freed("bias"))
            mm(bank("bias")[0:H_D, :], rb, oh).then_inc(*made("bias"))

            def project(name, sname, l, w, i=0):
                pe.wait_ge(*freed(name, l, i))
                for t in range(NT):
                    for k in range(KT):
                        if name == "c0" and t == 0:
                            pe.wait_ge(*after("xg", l, k))
                        last = mm(bank(name)[:, t * CH:t * CH + w.shape[2]], XN[:, k, t * P:(t + 1) * P], w[:, k, :],
                                  k == 0, k == KT - 1)
                last.then_inc(*made(name))

            def attention(kind, n_heads, per, l):
                for s in range(n_heads + 3):
                    if s < n_heads and s % per == 0:
                        u = s // per
                        name = f"{kind}t{u}"
                        pe.wait_ge(*freed(name, l))
                        for n in range(2):
                            for t in range(NT):
                                if kind == "a":
                                    src = (q_mla, k_mla)[n][:, t, u * QK_A:(u + 1) * QK_A]
                                    o = bank(name)[0:QK_A, (2 * n + t) * P:(2 * n + t + 1) * P]
                                else:
                                    src = PR[:, t, (DQ, DK)[n] + u * P:(DQ, DK)[n] + (u + 1) * P]
                                    o = bank(name)[:, (2 * n + t) * P:(2 * n + t + 1) * P]
                                last = pe.transpose(o, src, ident)
                        last.then_inc(*made(name))
                    if 1 <= s <= n_heads:
                        h = s - 1
                        name = f"{kind}s{h}"
                        lo, kd = (0, QK_A) if kind == "a" else (HD_D * (h % 2), HD_D)
                        qk = qkT[lo:lo + kd, h // per % 2, :]
                        pe.wait_ge(*freed(name, l))
                        pe.wait_ge(*copied(f"{kind}t{h // per}", l))
                        for t in range(NT):
                            o = bank(name)[:, t * S:(t + 1) * S]
                            if kind == "d":
                                mm(o, flip, BIAS[:, h, P - t * P:P - t * P + S], True, False)
                            last = mm(o, qk[:, t * P:(t + 1) * P], qk[:, S:2 * S], kind == "a", True)
                        last.then_inc(*made(name))
                    if 2 <= s <= n_heads + 1:
                        h = s - 2
                        name = f"{kind}p{h}"
                        pe.wait_ge(*freed(name, l))
                        pe.wait_ge(*copied(f"{kind}s{h}", l))
                        for kt in range(NT):
                            for t in range(NT):
                                last = pe.transpose(bank(name)[:, (kt * NT + t) * P:(kt * NT + t + 1) * P],
                                                    prob[:, h % 2, t, kt * P:(kt + 1) * P], ident)
                        last.then_inc(*made(name))
                    if s >= 3:
                        h = s - 3
                        name = f"{kind}o{h}"
                        pe.wait_ge(*freed(name, l))
                        pe.wait_ge(*copied(f"{kind}p{h}", l))
                        for t in range(NT):
                            for kt in range(NT):
                                v = v_mla[:, kt, h * DV_A:(h + 1) * DV_A] if kind == "a" else PR[:, kt, DV + h * HD_D:DV + (h + 1) * HD_D]
                                last = mm(bank(name)[:, t * 64:(t + 1) * 64], pT[:, h % 2, kt, t * P:(t + 1) * P], v,
                                          kt == 0, kt == NT - 1)
                        last.then_inc(*made(name))

            with pe.Fori(0, DEPTH) as l:
                pe.wait_ge(*freed("ssq", l))
                pe.wait_ge(*after("sq", l, 3))
                for t in range(NT):
                    for k in range(KT):
                        last = mm(bank("ssq")[:, t:t + 1], SQ[:, k, t * P:(t + 1) * P], ones[:, 0:1], k == 0, k == KT - 1)
                last.then_inc(*made("ssq"))
                for j in range(3):
                    w = slot(f"c{j}")
                    if j < 2:
                        pe.wait_ge(*loaded(f"c{j}", l))
                        project(f"c{j}", f"c{j}", l, w.rearrange("p (k c) -> p k c", k=KT))
                    else:
                        pe.wait_ge(c2_full, (l + 1) * 32)
                        project("c2", "c2", l, w[:, 0:KT * 48].rearrange("p (k c) -> p k c", k=KT))
                pe.wait_ge(*after("lat_n", l))
                for t in range(NT):
                    pe.wait_ge(*freed(f"lat{t}", l))
                    for k in range(4):
                        last = pe.transpose(bank(f"lat{t}")[:, k * P:(k + 1) * P], PR[:, t, k * P:(k + 1) * P], ident)
                    last.then_inc(*made(f"lat{t}"))
                pe.wait_ge(up_full, (l + 1) * 32)
                pe.wait_ge(*copied("lat1", l))
                for t in range(NT):
                    for j in range(4):
                        name = f"up{t}{j}"
                        pe.wait_ge(*freed(name, l))
                        if j < 2:
                            for k in range(3):
                                last = mm(bank(name)[:, 0:384], latT[:, k, t * P:(t + 1) * P],
                                          slot("up")[:, k * W_D + j * 384:k * W_D + (j + 1) * 384], k == 0, k == 2)
                        else:
                            last = mm(bank(name), latT[:, 3, t * P:(t + 1) * P],
                                      slot("up")[:, 3 * W_D + (j - 2) * 512:3 * W_D + (j - 1) * 512])
                        last.then_inc(*made(name))
                with pe.Fori(0, MAIN_ITERS - 1) as i:
                    for j in range(NSLOT):
                        pe.wait_ge(*loaded(f"m{j}", l, i))
                        project(f"m{j}", f"m{j}", l, slot(f"m{j}").rearrange("p (k c) -> p k c", k=KT), i)
                pe.wait_ge(*after("a_n", l))
                attention("a", H_A, 1, l)
                for j in range(NSLOT):
                    pe.wait_ge(*loaded(f"z{j}", l))
                    project(f"z{j}", f"z{j}", l, slot(f"z{j}").rearrange("p (k c) -> p k c", k=KT))
                pe.wait_ge(*after("d_n", l))
                pe.wait_ge(bias_out, 32)
                attention("d", H_D, 2, l)

                pe.wait_ge(*after("gate_b", l))
                for d in range(2):
                    pe.wait_ge(*freed(f"rows{d}", l))
                    for n in range(2):
                        for t in range(NT):
                            g = MG + (2 * d + n) * H_M
                            last = mm(bank(f"rows{d}")[0:H_M, n * S + t * P:n * S + (t + 1) * P], PR[:, t, g:g + H_M], ident)
                    last.then_inc(*made(f"rows{d}"))
                for m in range(NCB // 2):
                    name = f"mu{m}"
                    pe.wait_ge(*freed(name, l))
                    for b in range(2):
                        for t in range(NT):
                            c = MU + (2 * m + b) * CB
                            last = pe.transpose(bank(name)[0:CB, b * S + t * P:b * S + (t + 1) * P], PR[:, t, c:c + CB], ident)
                    last.then_inc(*made(name))
                pe.wait_ge(*freed("gcols", l))
                for d in range(2):
                    pe.wait_ge(*after("rows_ready", l, d))
                    for n in range(2):
                        for t in range(NT):
                            c = ((n * 2 + d) * NT + t) * H_M
                            last = mm(bank("gcols")[:, c:c + H_M], grow(d, (2, 4)[n])[:, t * P:(t + 1) * P], K[0:H_M, 0:H_M])
                last.then_inc(*made("gcols"))
                pe.wait_ge(mw_full, (l + 1) * 32)
                for h in range(H_M + 1):
                    if h < H_M:
                        for n, c in enumerate("qk"):
                            name = f"m{c}{h}"
                            pe.wait_ge(*freed(name, l))
                            if n == 0:
                                pe.wait_ge(*after("uc_ready", l, h))
                            for e in range(2):
                                for b in range(2):
                                    w = (n * NCB + 2 * h + b) * HD_M + e * CB
                                    last = mm(bank(name)[0:CB, e * S:(e + 1) * S], slot("mw")[0:CB, w:w + CB],
                                              uc[:, 2 * h + b, :], b == 0, b == 1)
                            last.then_inc(*made(name))
                        for d in range(2):
                            name = f"w{h}{d}"
                            pe.wait_ge(*freed(name, l))
                            pick = K[0:H_M, h:h + 1].to_broadcast([H_M, P])
                            neg_m = grow(d, 0)
                            o = bank(name)
                            if d == 0:
                                mm(o[:, 0:S], pick, neg_m, True, False)
                                mm(o[:, 0:P], ident, mask, False, True)
                                mm(o[:, S:S + P], pick, neg_m[:, P:S], True, False)
                                last = mm(o[:, S:S + P], ident, mask, False, True)
                            else:
                                mm(o[:, 0:P], pick, neg_m[:, 0:P], True, False)
                                mm(o[:, 0:P], mask, ident, False, True)
                                mm(o[:, P:P + S], pick, neg_m, True, False)
                                last = mm(o[:, S:S + P], mask, ident, False, True)
                            last.then_inc(*made(name))
                        name = f"ms{h}"
                        pe.wait_ge(*freed(name, l))
                        pe.wait_ge(*copied(f"mq{h}", l))
                        pe.wait_ge(*copied(f"mk{h}", l))
                        for s in range(NT):
                            for e in range(2):
                                last = mm(bank(name)[:, s * S:(s + 1) * S], mqk[:, h % 2, 1, e * S + s * P:e * S + (s + 1) * P],
                                          mqk[:, h % 2, 0, e * S:(e + 1) * S], e == 0, e == 1)
                        last.then_inc(*made(name))
                    if h >= 1:
                        g = h - 1
                        pe.wait_ge(*copied(f"ms{g}", l))
                        for d in range(2):
                            name = f"n{g}{d}"
                            pe.wait_ge(*freed(name, l))
                            of = ((0, ((0, 0),)), (1, ((1, 0), (2, 1)))) if d == 0 else ((0, ((0, 0), (1, 1))), (1, ((2, 1),)))
                            for t, parts in of:
                                for lo, n, src in ((0, HD_M, "v"), (HD_M, 1, "1")):
                                    for j, (blk, s) in enumerate(parts):
                                        rhs = PR[:, s, MV + g * HD_M:MV + (g + 1) * HD_M] if src == "v" else ones[:, 0:1]
                                        last = mm(bank(name)[:, t * S + lo:t * S + lo + n],
                                                  decay[:, g % 2, d, blk * P:(blk + 1) * P], rhs,
                                                  j == 0, j == len(parts) - 1)
                            last.then_inc(*made(name))
                for j in range(KT // 2):
                    name = f"y{j}"
                    pe.wait_ge(*freed(name, l))
                    if j == 0:
                        pe.wait_ge(*copied(f"do{H_D - 1}", l))
                    if j == 5:
                        pe.wait_ge(*after("y_ml", l))
                    for q in range(2):
                        kk = 2 * j + q
                        c = kk * P if kk < 4 else DQ + (kk - 4) * P if kk < 10 else MU + (kk - 10) * P
                        for t in range(NT):
                            last = pe.transpose(bank(name)[:, q * S + t * P:q * S + (t + 1) * P], PR[:, t, c:c + P], ident)
                    last.then_inc(*made(name))
                for j in range(N_OUT):
                    name = f"o{j}"
                    w = slot(name).rearrange("p (k c) -> p k c", k=KT)
                    pe.wait_ge(*loaded(name, l))
                    pe.wait_ge(*freed(name, l))
                    if j == 0:
                        for q in (KT // 2 - 2, KT // 2 - 1):
                            pe.wait_ge(*copied(f"y{q}", l))
                    for q in range(2):
                        for k in range(KT):
                            last = mm(bank(name)[:, q * S:(q + 1) * S], w[:, k, q * P:(q + 1) * P], XN[:, k, :], k == 0, k == KT - 1)
                    last.then_inc(*made(name))
                pe.wait_ge(*freed("ssq2", l))
                pe.wait_ge(*after("sq2", l, 3))
                for k in range(KT):
                    last = mm(bank("ssq2")[:, 0:S], ones[:, 0:P], SQ[:, k, :], k == 0, k == KT - 1)
                last.then_inc(*made("ssq2"))
                pe.wait_ge(*freed("route", l))
                pe.wait_ge(rw_in, (l + 1) * 32)
                pe.wait_ge(*after("xn2", l, KT - 1))
                for t in range(NT):
                    for k in range(KT):
                        last = mm(bank("route")[:, t * 32:t * 32 + NG + NE], XN[:, k, t * P:(t + 1) * P], w_rt[:, k, :], k == 0, k == KT - 1)
                last.then_inc(*made("route"))
                pe.wait_ge(*freed("combT", l))
                pe.wait_ge(*after("comb", l))
                for t in range(NT):
                    last = mm(bank("combT")[0:NE, t * P:(t + 1) * P], rt[:, 5, t, :], ident)
                last.then_inc(*made("combT"))
                pe.wait_ge(*copied("combT", l))
                for j in range(NE // 2):
                    name = f"cb{j}"
                    pe.wait_ge(*freed(name, l))
                    for q in range(2):
                        e = 2 * j + q
                        last = mm(bank(name)[:, q * S:(q + 1) * S], K[0:NE, e:e + 1].to_broadcast([NE, P]), combT[:, :])
                    last.then_inc(*made(name))
                with pe.Fori(0, NE) as e:
                    for half in range(2):
                        for n in "gu":
                            name = f"{n}{half}"
                            w = slot(name).rearrange("p (k c) -> p k c", k=KT)
                            pe.wait_ge(*loaded(name, l, e))
                            pe.wait_ge(*freed(name, l, e))
                            for q in range(2):
                                for k in range(KT):
                                    last = mm(bank(name)[:, q * S:(q + 1) * S], w[:, k, q * P:(q + 1) * P], XN[:, k, :], k == 0, k == KT - 1)
                            last.then_inc(*made(name))
                    s, v = after("h_gated", l, 1)
                    pe.wait_ge(s, v + e * 2)
                    for j in range(KT // 2):
                        name = f"dn{j}"
                        if j % 4 == 0:
                            pe.wait_ge(*loaded(f"d{j // 4}", l, e))
                            w = slot(f"d{j // 4}").rearrange("p (k c) -> p k c", k=4)
                        pe.wait_ge(*freed(name, l, e))
                        for q in range(2):
                            c = (2 * (j % 4) + q) * P
                            for k in range(4):
                                last = mm(bank(name)[:, q * S:(q + 1) * S], w[:, k, c:c + P], hT[:, k, :], k == 0, k == 3)
                        last.then_inc(*made(name))
            pe.wait_ge(*copied("dn7", DEPTH - 1, NE - 1))
            for t in range(NT):
                for g in range(KT // 4):
                    name = f"f{t * KT // 4 + g}"
                    pe.wait_ge(*freed(name))
                    for q in range(4):
                        last = pe.transpose(bank(name)[:, q * P:(q + 1) * P], X[:, 4 * g + q, t * P:(t + 1) * P], ident)
                    last.then_inc(*made(name))

        def pcol(r):
            return col[:, r:r + 1]

        def pcol96(r):
            return col96[:, r:r + 1]

        def t_h(ap, h):
            return ap.rearrange("p t (h w) -> p t h w", h=h)

        def main_dst(name, i=0):
            j = int(name[1:]) + NSLOT * (MAIN_ITERS - 1 if name[0] == "z" else i)
            return DQ + j * CH

        qv, kv = t_h(q_mla, H_A), t_h(k_mla, H_A)
        MAGIC = 12582912.0
        PI = float(np.pi)
        C1 = 6.28125
        C2 = float(np.round((2 * np.pi - C1) * 2 ** 20) / 2 ** 20)
        C3 = float(2 * np.pi - C1 - C2)

        @block.vector
        def _(dve):
            own = Steps(dve, dve_steps, DVE_PRE, DVE_LAYER)

            def do(ins):
                own.did(ins)
                own.wait()

            dve.memset(ones[:, :], 1.0).then_inc(ones_set, 1)
            dve.memset(eps[:, :], EPS).then_inc(ones_set, 1)
            for j in range(0, NT * KT // 4, 2):
                t, g = j // (KT // 4), j % (KT // 4)
                dve.wait_ge(*ready(f"x{j}"))
                dve.tensor_copy(X[:, 4 * g:4 * g + 4, t * P:(t + 1) * P],
                                bank(f"x{j}").rearrange("p (k s) -> p k s", k=4)).then_inc(*read(f"x{j}"))
            for l in range(DEPTH):
                dve.wait_ge(*ready(f"par{l}"))
                dve.tensor_copy(par[:, l, :], bank(f"par{l}")[:, 0:N_ROW]).then_inc(*read(f"par{l}"))
                dve.wait_ge(*ready(f"par96{l}"))
                dve.tensor_copy(par96[:, l, :], bank(f"par96{l}")[0:CB, 0:N_ROW96]).then_inc(*read(f"par96{l}"))
            dve.wait_ge(bias_in, 48)
            dve.wait_ge(*ready("bias"))
            dve.tensor_tensor(fbias, bank("bias")[0:H_D, :], lnc, ALU.add).then_inc(*read("bias"))
            dve.wait_ge(pos_in, 16)
            dve.wait_ge(const_in, 16)
            do(dve.tensor_copy(pos_f[:, :], pos_i[:, :]))
            for t in range(NT):
                own.did(dve.tensor_scalar(ang[:, 0, t, :], K[:, K_FREQ:K_FREQ + HALF], pos_f[:, t:t + 1], None, ALU.mult))
            own.wait()
            for n, turn in enumerate((0.25, 0.0)):
                k, r = ang[:, 1, :, :], ang[:, 2 + n, :, :]
                do(dve.tensor_scalar(k, ang[:, 0, :, :], 1.0 / (2 * PI), turn, ALU.mult, ALU.add))
                do(dve.tensor_scalar(k, k, MAGIC, None, ALU.add))
                do(dve.tensor_scalar(k, k, -MAGIC, None, ALU.add))
                do(dve.scalar_tensor_tensor(r, k, -C1, ang[:, 0, :, :], ALU.mult, ALU.add))
                do(dve.scalar_tensor_tensor(r, k, -C2, r, ALU.mult, ALU.add))
                do(dve.scalar_tensor_tensor(r, k, -C3, r, ALU.mult, ALU.add))
                do(dve.tensor_scalar(r, r, turn * 2 * PI, PI, ALU.add, ALU.min))
                ins = dve.tensor_scalar(r, r, -PI, None, ALU.max)
                ins.then_inc(ang_set, 1)
            for j in range(1, NT * KT // 4, 2):
                dve.wait_ge(*copied(f"x{j}"))
            for j in range(0, NT * KT // 4, 2):
                dve.wait_ge(*copied(f"x{j}"))
            dve.wait_ge(*copied(f"par96{DEPTH - 1}"))
            dve.wait_ge(par_in, N_PAR)

            def keep(name, l, lo, w, i=0):
                dve.wait_ge(*ready(name, l, i))
                for t in range(NT):
                    ins = dve.tensor_scalar(PR[:, t, lo:lo + w], bank(name)[:, t * CH:t * CH + w], rstd_x[:, t:t + 1], None, ALU.mult)
                ins.then_inc(*read(name))

            def max_of(name, l, b, scale):
                dve.wait_ge(*ready(name, l))
                do(dve.tensor_reduce(mx[:, b, :], bank(name).rearrange("p (t n) -> p t n", t=NT), AX, ALU.max))
                dve.tensor_scalar(nmx[:, b, :], mx[:, b, :], -scale, None, ALU.mult).then_inc(*signal("nmax"))

            def attention(kind, n_heads, scale, l):
                for s in range(1, n_heads + 2):
                    if s <= n_heads:
                        max_of(f"{kind}s{s - 1}", l, (s - 1) % 2, scale)
                    if s >= 2:
                        h = s - 2
                        dve.wait_ge(*copied(f"{kind}s{h}", l))
                        dve.reciprocal(rs[:, h % 4, :], psum_p[:, h % 2, :]).then_inc(*signal("rsum"))
                        dve.wait_ge(*ready(f"{kind}p{h}", l))
                        dve.tensor_copy(pT[:, h % 2, :, :].rearrange("p t n -> p (t n)"), bank(f"{kind}p{h}")).then_inc(*read(f"{kind}p{h}"))

            with dve.Fori(0, DEPTH) as l:
                own.enter_layer(l)

                def bias_row(lo, n):
                    return brow[:, bass.ds(l, 1), lo:lo + n].to_broadcast([P, NT, n])

                dve.wait_ge(psum_free[BANKS.where("dn7")], BANKS.count["pre"][7] + l * BANKS.count["layer"][7])
                dve.tensor_scalar(col[:, :].unsqueeze(1), par[:, bass.ds(l, 1), :], 1.0, None, ALU.mult).then_inc(*signal("cols"))
                dve.tensor_scalar(col96[:, :].unsqueeze(1), par96[:, bass.ds(l, 1), :], 1.0, None, ALU.mult).then_inc(*signal("cols"))
                dve.wait_ge(*after("cols", l, 1))
                for k in range(KT):
                    dve.tensor_scalar(XN[:, k, :], X[:, k, :], pcol(R_MIX + k), None, ALU.mult).then_inc(*signal("xg"))
                dve.wait_ge(*copied("ssq", l))
                dve.reciprocal(rstd_x[:, :], std_x[:, :]).then_inc(*signal("rstd_x"))
                dve.wait_ge(*after("rstd_x", l))
                keep("c1", l, CH, CH)
                keep("c2", l, 2 * CH, 48)
                dve.wait_ge(*after("lat_std", l))
                do(dve.reciprocal(rstd_lat[:, :, :], std_lat[:, :, :]))
                for t in range(NT):
                    for n, (lo, w) in enumerate(((CQ, QR), (CKV, KVR))):
                        ins = dve.tensor_scalar(PR[:, t, lo:lo + w], PR[:, t, lo:lo + w], rstd_lat[:, n, t:t + 1], None, ALU.mult)
                        if t < NT - 1 or n == 0:
                            own.did(ins)
                        else:
                            ins.then_inc(*signal("lat_n"))
                for t in range(NT):
                    dve.wait_ge(*ready(f"lat{t}", l))
                    for k in range(4):
                        ins = dve.tensor_scalar(latT[:, k, t * P:(t + 1) * P], bank(f"lat{t}")[:, k * P:(k + 1) * P], pcol(R_CQ + k), None, ALU.mult)
                    ins.then_inc(*read(f"lat{t}"))
                dve.wait_ge(*copied("c2", l))
                dve.tensor_tensor(PR[:, :, MG:MG + 16], PR[:, :, MG:MG + 16], bias_row(0, 16), ALU.add).then_inc(*signal("gate_b"))
                dve.wait_ge(ang_set, 2 + 1)
                kr1, kr2 = PR[:, :, KR:KR + HALF], PR[:, :, KR + HALF:KR + ROPE]
                for n, (x, c) in enumerate(((kr1, 0), (kr2, 1), (kr1, 1), (kr2, 0))):
                    own.did(dve.tensor_tensor(rt[:, n, :, :], x, cs[:, c, :, :], ALU.mult))
                own.wait()
                own.did(dve.tensor_tensor(rt[:, 4, :, :], rt[:, 0, :, :], rt[:, 1, :, :], ALU.subtract))
                do(dve.tensor_tensor(rt[:, 5, :, :], rt[:, 2, :, :], rt[:, 3, :, :], ALU.add))
                for n in range(2):
                    own.did(dve.tensor_copy(kv[:, :, :, NOPE + n * HALF:NOPE + (n + 1) * HALF],
                                            rt[:, 4 + n, :, :].unsqueeze(2).to_broadcast([P, NT, H_A, HALF])))
                for t in range(NT):
                    for j in (2, 3):
                        name = f"up{t}{j}"
                        h = 4 * (j - 2)
                        src = bank(name).rearrange("p (h w) -> p h w", h=4)
                        dve.wait_ge(*ready(name, l))
                        dve.tensor_copy(kv[:, t, h:h + 4, 0:NOPE], src[:, :, 0:NOPE])
                        dve.tensor_copy(v_mla[:, t, h * DV_A:(h + 4) * DV_A].rearrange("p (h w) -> p h w", h=4),
                                        src[:, :, NOPE:]).then_inc(*read(name))
                dve.wait_ge(*copied("up01", l))
                dve.wait_ge(*copied("up11", l))
                own.wait()
                x1, x2 = qv[:, :, :, NOPE:NOPE + HALF], qv[:, :, :, NOPE + HALF:]
                cos, sin = (cs[:, n, :, :].unsqueeze(2).to_broadcast([P, NT, H_A, HALF]) for n in range(2))
                for n, (x, c) in enumerate(((x1, cos), (x2, sin), (x1, sin), (x2, cos))):
                    own.did(dve.tensor_tensor(rtmp[:, n, :, :, :], x, c, ALU.mult))
                own.wait()
                own.did(dve.tensor_tensor(x1, rtmp[:, 0, :, :, :], rtmp[:, 1, :, :, :], ALU.subtract))
                dve.tensor_tensor(x2, rtmp[:, 2, :, :, :], rtmp[:, 3, :, :, :], ALU.add).then_inc(*signal("a_roped"))
                dve.wait_ge(*after("a_sq", l))
                own.did(dve.tensor_reduce(ss_a[:, 0, :, :], t_h(PR[:, :, DV:DV + W_D], H_A), AX, ALU.add))
                dve.tensor_reduce(ss_a[:, 1, :, :], t_h(PR[:, :, MU:MU + W_M], H_A), AX, ALU.add).then_inc(*signal("a_ss"))
                dve.wait_ge(*after("a_std", l))
                do(dve.reciprocal(rstd_a[:, :, :, :], std_a[:, :, :, :]))
                own.did(dve.tensor_tensor(qv, qv, rstd_a[:, 0, :, :].unsqueeze(3).to_broadcast([P, NT, H_A, QK_A]), ALU.mult))
                dve.tensor_tensor(kv, kv, rstd_a[:, 1, :, :].unsqueeze(3).to_broadcast([P, NT, H_A, QK_A]), ALU.mult).then_inc(*signal("a_n"))
                for j in range(1, NSLOT, 2):
                    keep(f"m{j}", l, main_dst(f"m{j}", 0), CH, 0)
                dve.wait_ge(*after("d_sq", l))
                own.did(dve.tensor_reduce(ss_d[:, 0, :, :], t_h(PR[:, :, DV:DV + W_D], H_D), AX, ALU.add))
                dve.tensor_reduce(ss_d[:, 1, :, :], t_h(PR[:, :, MU:MU + W_M], H_D), AX, ALU.add).then_inc(*signal("d_ss"))
                dve.wait_ge(*after("d_std", l))
                do(dve.reciprocal(rstd_d[:, :, :, :], std_d[:, :, :, :]))
                do(dve.tensor_scalar(rstd_d[:, 0, :, :], rstd_d[:, 0, :, :], HD_D ** -0.5, None, ALU.mult))
                for n, lo in enumerate((DQ, DK)):
                    w = t_h(PR[:, :, lo:lo + W_D], H_D)
                    ins = dve.tensor_tensor(w, w, rstd_d[:, n, :, :].unsqueeze(3).to_broadcast([P, NT, H_D, HD_D]), ALU.mult)
                    if n == 0:
                        own.did(ins)
                    else:
                        ins.then_inc(*signal("d_n"))
                for j in range(1, NSLOT, 2):
                    keep(f"m{j}", l, main_dst(f"m{j}", 1), CH, 1)
                attention("a", H_A, QK_A ** -0.5, l)
                for j in range(1, NSLOT, 2):
                    keep(f"z{j}", l, main_dst(f"z{j}"), CH)
                attention("d", H_D, 1.0, l)

                for d in range(2):
                    name = f"rows{d}"
                    g_i, g_f = bank(name)[0:H_M, 0:S], bank(name)[0:H_M, S:2 * S]

                    def way(r):
                        return r if d == 0 else r[:, ::-1]

                    dve.wait_ge(*ready(name, l))
                    dve.wait_ge(*after("gate_ln", l, d))
                    do(dve.scalar_tensor_tensor(grow(d, 3), g_f, 0.0, grow(d, 0), ALU.min, ALU.subtract))
                    do(dve.tensor_tensor_scan(way(grow(d, 1)), ones[0:H_M, 0:1].to_broadcast([H_M, S]), way(grow(d, 3)), 0.0, ALU.mult, ALU.add))
                    dve.tensor_tensor(grow(d, 2), g_i, grow(d, 1), ALU.subtract).then_inc(*read(name))
                    dve.wait_ge(*copied(name, l))
                    do(dve.tensor_tensor_scan(way(grow(d, 3)), way(grow(d, 2)), way(grow(d, 2)), 0.0, ALU.max, ALU.max))
                    own.did(dve.tensor_scalar(grow(d, 0), grow(d, 3), -1.0, None, ALU.mult))
                    dve.scalar_tensor_tensor(grow(d, 4), grow(d, 1), -1.0, grow(d, 3), ALU.mult, ALU.subtract).then_inc(*signal("rows_ready"))
                for m in range(NCB // 2):
                    name = f"mu{m}"
                    dve.wait_ge(*ready(name, l))
                    for j in (2, 0, 1, 3, 4):
                        s = j - TAPS // 2
                        lo, hi = max(0, -s), S - max(0, s)
                        for b in range(2):
                            c = 2 * m + b
                            src = bank(name)[0:CB, b * S:(b + 1) * S]
                            if j == 2:
                                ins = dve.tensor_scalar(uc[:, c, :], src, pcol96(R_CW + j * NCB + c), pcol96(R_CB + c), ALU.mult, ALU.add)
                            else:
                                ins = dve.scalar_tensor_tensor(uc[:, c, lo:hi], src[:, lo + s:hi + s], pcol96(R_CW + j * NCB + c),
                                                               uc[:, c, lo:hi], ALU.mult, ALU.add)
                            if j == 4 and b == 1:
                                ins.then_inc(*read(name))
                            else:
                                own.did(ins)
                        if j != 4:
                            own.wait()
                dve.wait_ge(*ready("gcols", l))
                dve.tensor_copy(gcol[:, :, :, :, :].rearrange("p n d t h -> p (n d t h)"), bank("gcols")[:, 0:32]).then_inc(*read("gcols"))
                for h in range(H_M + 1):
                    if h < H_M:
                        dve.wait_ge(*ready(f"mk{h}", l))
                        dve.tensor_scalar(mqk[:, h % 2, 1, :], bank(f"mk{h}")[0:CB, :], HD_M ** -0.5, None, ALU.mult).then_inc(*read(f"mk{h}"))
                        dve.wait_ge(*ready(f"ms{h}", l))
                        dve.wait_ge(*copied(f"w{h}0", l))
                        dve.wait_ge(*copied(f"w{h}1", l))
                        for d, lo, hi, src in ((0, 0, S, 0), (0, S, S + P, S + P), (1, 0, P, 0), (1, P, P + S, S)):
                            w = decay[:, h % 2, d, lo:hi]
                            ins = dve.tensor_tensor(w, w, bank(f"ms{h}")[:, src:src + hi - lo], ALU.mult)
                        ins.then_inc(*read(f"ms{h}"))
                    if h >= 1:
                        g = h - 1
                        dens = [bank(f"n{g}{d}").rearrange("p (t n) -> p t n", t=NT)[:, :, HD_M] for d in range(2)]
                        for d in range(2):
                            dve.wait_ge(*ready(f"n{g}{d}", l))
                            own.did(dve.tensor_scalar(dn[:, 1, d, :], dens[d], -1.0, None, ALU.mult))
                        own.wait()
                        for d in range(2):
                            own.did(dve.tensor_tensor(dn[:, 0, d, :], dn[:, 1, d, :], dens[d], ALU.max))
                        dve.wait_ge(*after("em_ready", l))
                        own.wait()
                        do(dve.tensor_tensor(dn[:, 0, :, :], dn[:, 0, :, :], em[:, :, :, g], ALU.max))
                        dve.reciprocal(dn[:, 1, :, :], dn[:, 0, :, :]).then_inc(*signal("r_ready"))
                        dve.wait_ge(*after("r_ready", l, g))
                        dve.wait_ge(*copied(f"n{g}0", l))
                        for t in range(NT):
                            h_row = PR[:, t, MU + g * HD_M:MU + (g + 1) * HD_M]
                            ins = dve.scalar_tensor_tensor(h_row, bank(f"n{g}1")[:, t * S:t * S + HD_M], dn[:, 1, 1, t:t + 1], h_row, ALU.mult, ALU.add)
                        ins.then_inc(*read(f"n{g}1"))
                dve.wait_ge(*after("m_std", l))
                do(dve.reciprocal(rstd_m[:, :, :], std_m[:, :, :]))
                for t in range(NT):
                    for h in range(H_M):
                        y, o = (PR[:, t, c + h * HD_M:c + (h + 1) * HD_M] for c in (MU, MO))
                        ins = dve.scalar_tensor_tensor(y, y, rstd_m[:, h, t:t + 1], o, ALU.mult, ALU.mult)
                        if t == NT - 1 and h == H_M - 1:
                            ins.then_inc(*signal("y_ml"))
                for j in range(1, KT // 2, 2):
                    dve.wait_ge(*ready(f"y{j}", l))
                    for q in range(2):
                        kk = 2 * j + q
                        src = bank(f"y{j}")[:, q * S:(q + 1) * S]
                        if kk < 10:
                            ins = dve.tensor_copy(XN[:, kk, :], src)
                        else:
                            ins = dve.tensor_scalar(XN[:, kk, :], src, pcol(R_MLO + kk - 10), None, ALU.mult)
                    ins.then_inc(*read(f"y{j}"))
                for j in range(N_OUT):
                    dve.wait_ge(*ready(f"o{j}", l))
                    x = X[:, 2 * j:2 * j + 2, :].rearrange("p k s -> p (k s)")
                    dve.tensor_tensor(x, x, bank(f"o{j}"), ALU.add).then_inc(*read(f"o{j}"))
                std2, rstd2 = scr[:, 1024:1280], scr[:, 1280:1536]
                dve.wait_ge(*copied("ssq2", l))
                do(dve.reciprocal(rstd2, std2))
                for k in range(KT):
                    dve.scalar_tensor_tensor(XN[:, k, :], X[:, k, :], pcol(R_FFN + k), rstd2, ALU.mult, ALU.mult).then_inc(*signal("xn2"))
                dve.wait_ge(*ready("route", l))
                dve.tensor_tensor(lg[:, :, :], bank("route")[:, 0:64].rearrange("p (t n) -> p t n", t=NT)[:, :, 0:NG + NE],
                                  bias_row(16, NG + NE), ALU.add).then_inc(*read("route"))
                dve.wait_ge(*copied("route", l))
                g4, e16 = lg[:, :, 0:NG], lg[:, :, NG:]

                def over(ap, n):
                    return ap.unsqueeze(2).to_broadcast([P, NT, n])

                def key_row(lo, n):
                    return K[:, lo:lo + n].unsqueeze(1).to_broadcast([P, NT, n])

                def first_of(o, x, top, keys, n):
                    do(dve.tensor_tensor(o, x, over(top, n), ALU.is_equal))
                    do(dve.tensor_tensor(o, o, keys, ALU.mult))
                    do(dve.tensor_reduce(rs1[:, 3, :], o, AX, ALU.max))
                    do(dve.tensor_tensor(o, o, over(rs1[:, 3, :], n), ALU.is_equal))

                do(dve.tensor_reduce(rs1[:, 0, :], g4, AX, ALU.max))
                dve.tensor_tensor(rt[:, 0, :, 0:NG], g4, over(rs1[:, 0, :], NG), ALU.subtract).then_inc(*signal("e_in"))
                ohg = rt[:, 3, :, 0:NG]
                first_of(ohg, g4, rs1[:, 0, :], key_row(K_KEYG, NG), NG)
                do(dve.tensor_scalar(ohg, ohg, -1.0, -NEG, ALU.add, ALU.mult))
                dve.wait_ge(*after("e_exp", l, 0))
                do(dve.tensor_reduce(rs1[:, 1, :], rt[:, 1, :, 0:NG], AX, ALU.add))
                own.did(dve.reciprocal(rs1[:, 2, :], rs1[:, 1, :]))
                do(dve.tensor_tensor(rt[:, 4, :, :].rearrange("p t (g e) -> p t g e", g=NG), e16.rearrange("p t (g e) -> p t g e", g=NG),
                                     ohg.unsqueeze(3).to_broadcast([P, NT, NG, EPG]), ALU.add))
                do(dve.tensor_reduce(rs1[:, 4, :], rt[:, 4, :, :], AX, ALU.max))
                first_of(rt[:, 1, :, :], rt[:, 4, :, :], rs1[:, 4, :], key_row(K_KEYE, NE), NE)
                do(dve.scalar_tensor_tensor(rt[:, 4, :, :], rt[:, 1, :, :], 2 * NEG, rt[:, 4, :, :], ALU.mult, ALU.add))
                do(dve.tensor_reduce(rs1[:, 5, :], rt[:, 4, :, :], AX, ALU.max))
                dve.tensor_tensor(rs1[:, 6, :], rs1[:, 5, :], rs1[:, 4, :], ALU.subtract).then_inc(*signal("e_in"))
                first_of(rt[:, 2, :, :], rt[:, 4, :, :], rs1[:, 5, :], key_row(K_KEYE, NE), NE)
                dve.wait_ge(*after("e_exp", l, 1))
                do(dve.tensor_scalar(rs1[:, 3, :], rs1[:, 7, :], 1.0, None, ALU.add))
                do(dve.reciprocal(rs1[:, 0, :], rs1[:, 3, :]))
                do(dve.tensor_tensor(rs1[:, 0, :], rs1[:, 0, :], rs1[:, 2, :], ALU.mult))
                do(dve.tensor_tensor(rs1[:, 1, :], rs1[:, 0, :], rs1[:, 7, :], ALU.mult))
                own.did(dve.tensor_tensor(rt[:, 1, :, :], rt[:, 1, :, :], over(rs1[:, 0, :], NE), ALU.mult))
                do(dve.tensor_tensor(rt[:, 2, :, :], rt[:, 2, :, :], over(rs1[:, 1, :], NE), ALU.mult))
                dve.tensor_tensor(rt[:, 5, :, :], rt[:, 1, :, :], rt[:, 2, :, :], ALU.add).then_inc(*signal("comb"))
                dve.wait_ge(*ready("combT", l))
                dve.tensor_copy(combT[:, :], bank("combT")[0:NE, 0:S]).then_inc(*read("combT"))
                for j in range(1, NE // 2, 2):
                    dve.wait_ge(*ready(f"cb{j}", l))
                    dve.tensor_copy(combB[:, 2 * j:2 * j + 2, :].rearrange("p e s -> p (e s)"), bank(f"cb{j}")).then_inc(*read(f"cb{j}"))
                with dve.Fori(0, NE) as e:
                    dve.wait_ge(*copied(f"cb{NE // 2 - 1}", l))
                    dve.wait_ge(*copied(f"cb{NE // 2 - 2}", l))
                    for half in range(2):
                        dve.wait_ge(*copied(f"g{half}", l, e))
                        dve.wait_ge(*ready(f"u{half}", l, e))
                        h2 = hT[:, 2 * half:2 * half + 2, :]
                        dve.tensor_tensor(h2.rearrange("p k n -> p (k n)"), sg[:, half, :], bank(f"u{half}"), ALU.mult).then_inc(*read(f"u{half}"))
                        dve.wait_ge(*copied(f"u{half}", l, e))
                        dve.tensor_tensor(h2, h2, combB[:, bass.ds(e, 1), :].to_broadcast([P, 2, S]), ALU.mult).then_inc(*signal("h_gated"))
                    for j in range(KT // 2):
                        dve.wait_ge(*ready(f"dn{j}", l, e))
                        dve.wait_ge(*freed(f"dn{j}", l, e))
                        x = X[:, 2 * j:2 * j + 2, :].rearrange("p k s -> p (k s)")
                        dve.tensor_tensor(x, x, bank(f"dn{j}"), ALU.add).then_inc(*read(f"dn{j}"))
                own.leave_layer()
            for j in range(0, NT * KT // 4, 2):
                t, g = j // (KT // 4), j % (KT // 4)
                dve.wait_ge(*ready(f"f{j}"))
                dve.tensor_copy(PR[:, t, g * 512:(g + 1) * 512], bank(f"f{j}")).then_inc(*read(f"f{j}"))

        @block.scalar
        def _(act):
            own = Steps(act, act_steps, 0, ACT_LAYER)

            def do(ins):
                own.did(ins)
                own.wait()

            for j in range(1, NT * KT // 4, 2):
                t, g = j // (KT // 4), j % (KT // 4)
                act.wait_ge(*ready(f"x{j}"))
                act.activation(X[:, 4 * g:4 * g + 4, t * P:(t + 1) * P],
                               bank(f"x{j}").rearrange("p (k s) -> p k s", k=4), ACT.Copy).then_inc(*read(f"x{j}"))
            act.wait_ge(ones_set, 2)
            for n in range(2):
                act.wait_ge(ang_set, n + 1)
                ins = act.activation(cs[:, n, :, :], ang[:, 2 + n, :, :], ACT.Sin)
            ins.then_inc(ang_set, 1)
            for j in range(NT * KT // 4):
                act.wait_ge(*copied(f"x{j}"))
            act.wait_ge(*copied(f"par96{DEPTH - 1}"))

            def keep(name, l, lo, w, i=0):
                act.wait_ge(*ready(name, l, i))
                for t in range(NT):
                    ins = act.activation(PR[:, t, lo:lo + w], bank(name)[:, t * CH:t * CH + w], ACT.Copy, scale=rstd_x[:, t:t + 1])
                ins.then_inc(*read(name))

            with act.Fori(0, DEPTH) as l:
                own.enter_layer(l)

                def attention(kind, n_heads, per, scale, n_first, cols, out_col, w):
                    for s in range(n_heads + 3):
                        if s < n_heads and s % per == 0:
                            name = f"{kind}t{s // per}"
                            act.wait_ge(*ready(name, l))
                            for n in range(2):
                                ins = act.activation(qkT[0:w, s // per % 2, n * S:(n + 1) * S], bank(name)[0:w, n * S:(n + 1) * S],
                                                     ACT.Copy, scale=cols[n])
                            ins.then_inc(*read(name))
                        if 1 <= s <= n_heads:
                            h = s - 1
                            act.wait_ge(*after("nmax", l, n_first + h))
                            for t in range(NT):
                                ins = act.activation(prob[:, h % 2, t, :], bank(f"{kind}s{h}")[:, t * S:(t + 1) * S], ACT.Exp,
                                                     bias=nmx[:, h % 2, t:t + 1], scale=scale, accum_out=psum_p[:, h % 2, t:t + 1])
                            ins.then_inc(*read(f"{kind}s{h}"))
                        if s >= 3:
                            h = s - 3
                            act.wait_ge(*after("rsum", l, n_first + h))
                            act.wait_ge(*ready(f"{kind}o{h}", l))
                            for t in range(NT):
                                ins = act.activation(PR[:, t, out_col + h * 64:out_col + (h + 1) * 64], bank(f"{kind}o{h}")[:, t * 64:(t + 1) * 64],
                                                     ACT.Copy, scale=rs[:, h % 4, t:t + 1])
                            ins.then_inc(*read(f"{kind}o{h}"))

                act.wait_ge(psum_free[BANKS.where("dn7")], BANKS.count["pre"][7] + l * BANKS.count["layer"][7])
                for q in range(4):
                    act.activation(SQ[:, 4 * q:4 * q + 4, :].rearrange("p k s -> p (k s)"),
                                   X[:, 4 * q:4 * q + 4, :].rearrange("p k s -> p (k s)"), ACT.Square).then_inc(*signal("sq"))
                act.wait_ge(*ready("ssq", l))
                act.activation(std_x[:, :], bank("ssq")[:, 0:NT], ACT.Sqrt, bias=eps[:, 0:1], scale=1.0 / D).then_inc(*read("ssq"))
                act.wait_ge(*after("rstd_x", l))
                act.wait_ge(*after("cols", l, 1))
                keep("c0", l, 0, CH)
                act.wait_ge(*copied("c0", l))
                act.wait_ge(*copied("c1", l))
                for t in range(NT):
                    for n, (lo, w) in enumerate(((CQ, QR), (CKV, KVR))):
                        dump = scr[:, 1024 + t * 512 + lo:1024 + t * 512 + lo + w]
                        own.did(act.activation(dump, PR[:, t, lo:lo + w], ACT.Square, accum_out=ss_lat[:, n, t:t + 1]))
                own.wait()
                own.did(act.activation(std_lat[:, 0, :], ss_lat[:, 0, :], ACT.Sqrt, bias=eps[:, 0:1], scale=1.0 / QR))
                act.activation(std_lat[:, 1, :], ss_lat[:, 1, :], ACT.Sqrt, bias=eps[:, 0:1], scale=1.0 / KVR).then_inc(*signal("lat_std"))
                for t in range(NT):
                    for j in range(2):
                        name = f"up{t}{j}"
                        act.wait_ge(*ready(name, l))
                        act.activation(q_mla[:, t, j * 384:(j + 1) * 384], bank(name)[:, 0:384], ACT.Copy).then_inc(*read(name))
                act.wait_ge(*after("a_roped", l))
                own.did(act.activation(PR[:, :, DV:DV + W_D], q_mla, ACT.Square))
                act.activation(PR[:, :, MU:MU + W_M], k_mla, ACT.Square).then_inc(*signal("a_sq"))
                act.wait_ge(*after("a_ss", l))
                act.activation(std_a[:, :, :, :].rearrange("p n t h -> p (n t h)"), ss_a[:, :, :, :].rearrange("p n t h -> p (n t h)"), ACT.Sqrt, bias=eps[:, 0:1], scale=1.0 / QK_A).then_inc(*signal("a_std"))
                for j in range(0, NSLOT, 2):
                    keep(f"m{j}", l, main_dst(f"m{j}", 0), CH, 0)
                for j in range(NSLOT):
                    act.wait_ge(*copied(f"m{j}", l, 0))
                own.did(act.activation(PR[:, :, DV:DV + W_D], PR[:, :, DQ:DQ + W_D], ACT.Square))
                act.activation(PR[:, :, MU:MU + W_M], PR[:, :, DK:DK + W_D], ACT.Square).then_inc(*signal("d_sq"))
                act.wait_ge(*after("d_ss", l))
                act.activation(std_d[:, :, :, :].rearrange("p n t h -> p (n t h)"), ss_d[:, :, :, :].rearrange("p n t h -> p (n t h)"), ACT.Sqrt, bias=eps[:, 0:1], scale=1.0 / HD_D).then_inc(*signal("d_std"))
                for j in range(0, NSLOT, 2):
                    keep(f"m{j}", l, main_dst(f"m{j}", 1), CH, 1)
                act.wait_ge(bias_out, 16)
                attention("a", H_A, 1, QK_A ** -0.5, 0, (pcol96(R_AQ), pcol96(R_AK)), 0, QK_A)
                for j in range(0, NSLOT, 2):
                    keep(f"z{j}", l, main_dst(f"z{j}"), CH)
                attention("d", H_D, 2, 1.0, H_A, (pcol(R_DQ), pcol(R_DK)), DQ, P)

                for d in range(2):
                    act.wait_ge(*ready(f"rows{d}", l))
                    do(act.activation(grow(d, 0), bank(f"rows{d}")[0:H_M, S:2 * S], ACT.Abs))
                    do(act.activation(grow(d, 0), grow(d, 0), ACT.Exp, scale=-1.0))
                    act.activation(grow(d, 0), grow(d, 0), ACT.Ln, bias=1.0).then_inc(*signal("gate_ln"))
                act.wait_ge(*copied("gcols", l))
                act.activation(em[:, :, :, :].rearrange("p d t h -> p (d t h)"), gcol[:, 1, :, :, :].rearrange("p d t h -> p (d t h)"),
                               ACT.Exp).then_inc(*signal("em_ready"))
                for h in range(H_M):
                    act.wait_ge(*copied(f"mu{h}", l))
                    u = uc[:, 2 * h:2 * h + 2, :].rearrange("p b s -> p (b s)")
                    act.activation(u, u, ACT.Silu).then_inc(*signal("uc_ready"))
                for h in range(H_M + 1):
                    if h < H_M:
                        act.wait_ge(*ready(f"mq{h}", l))
                        act.activation(mqk[:, h % 2, 0, :], bank(f"mq{h}")[0:CB, :], ACT.Copy).then_inc(*read(f"mq{h}"))
                        for d, cuts in ((0, ((0, S, 0), (S, S + P, 1))), (1, ((0, P, 0), (P, P + S, 1)))):
                            act.wait_ge(*ready(f"w{h}{d}", l))
                            for lo, hi, s in cuts:
                                ins = act.activation(decay[:, h % 2, d, lo:hi], bank(f"w{h}{d}")[:, lo:hi], ACT.Exp, bias=gcol[:, 0, d, s, h:h + 1])
                            ins.then_inc(*read(f"w{h}{d}"))
                    if h >= 1:
                        g = h - 1
                        act.wait_ge(*after("r_ready", l, g))
                        for t in range(NT):
                            ins = act.activation(PR[:, t, MU + g * HD_M:MU + (g + 1) * HD_M], bank(f"n{g}0")[:, t * S:t * S + HD_M],
                                                 ACT.Copy, scale=dn[:, 1, 0, t:t + 1])
                        ins.then_inc(*read(f"n{g}0"))
                        act.wait_ge(*copied(f"n{g}1", l))
                        if g:
                            own.wait()
                        for t in range(NT):
                            own.did(act.activation(scr[:, 2048 + t * HD_M:2048 + (t + 1) * HD_M], PR[:, t, MU + g * HD_M:MU + (g + 1) * HD_M], ACT.Square,
                                                   accum_out=ss_m[:, g, t:t + 1]))
                own.wait()
                own.did(act.activation(std_m[:, :, :].rearrange("p h t -> p (h t)"), ss_m[:, :, :].rearrange("p h t -> p (h t)"), ACT.Sqrt, bias=eps[:, 0:1], scale=1.0 / HD_M))
                act.activation(PR[:, :, MO:MO + W_M], PR[:, :, MO:MO + W_M], ACT.Sigmoid).then_inc(*signal("m_std"))
                for j in range(0, KT // 2, 2):
                    act.wait_ge(*ready(f"y{j}", l))
                    for q in range(2):
                        kk = 2 * j + q
                        src = bank(f"y{j}")[:, q * S:(q + 1) * S]
                        if kk < 10:
                            ins = act.activation(XN[:, kk, :], src, ACT.Copy)
                        else:
                            ins = act.activation(XN[:, kk, :], src, ACT.Copy, scale=pcol(R_MLO + kk - 10))
                    ins.then_inc(*read(f"y{j}"))
                for q in range(4):
                    act.wait_ge(*copied(f"o{2 * q}", l))
                    act.wait_ge(*copied(f"o{2 * q + 1}", l))
                    act.activation(SQ[:, 4 * q:4 * q + 4, :].rearrange("p k s -> p (k s)"),
                                   X[:, 4 * q:4 * q + 4, :].rearrange("p k s -> p (k s)"), ACT.Square).then_inc(*signal("sq2"))
                act.wait_ge(*ready("ssq2", l))
                act.activation(scr[:, 1024:1280], bank("ssq2")[:, 0:S], ACT.Sqrt, bias=eps[:, 0:1], scale=1.0 / D).then_inc(*read("ssq2"))
                act.wait_ge(*after("e_in", l, 0))
                act.activation(rt[:, 1, :, 0:NG], rt[:, 0, :, 0:NG], ACT.Exp).then_inc(*signal("e_exp"))
                act.wait_ge(*after("e_in", l, 1))
                act.activation(rs1[:, 7, :], rs1[:, 6, :], ACT.Exp).then_inc(*signal("e_exp"))
                for j in range(0, NE // 2, 2):
                    act.wait_ge(*ready(f"cb{j}", l))
                    act.activation(combB[:, 2 * j:2 * j + 2, :].rearrange("p e s -> p (e s)"), bank(f"cb{j}"), ACT.Copy).then_inc(*read(f"cb{j}"))
                with act.Fori(0, NE) as e:
                    for half in range(2):
                        act.wait_ge(*ready(f"g{half}", l, e))
                        act.activation(sg[:, half, :], bank(f"g{half}"), ACT.Silu).then_inc(*read(f"g{half}"))
                own.leave_layer()
            for j in range(1, NT * KT // 4, 2):
                t, g = j // (KT // 4), j % (KT // 4)
                act.wait_ge(*ready(f"f{j}"))
                act.activation(PR[:, t, g * 512:(g + 1) * 512], bank(f"f{j}"), ACT.Copy).then_inc(*read(f"f{j}"))



INPUTS = ["x", "positions", "rel_bias", "norm_mix", "w_in", "mla_norm_cq", "mla_w_uq", "mla_norm_ckv", "mla_w_ukv",
          "mla_q_norm", "mla_k_norm", "dil_q_norm", "dil_k_norm", "ml_conv_w", "ml_conv_b", "ml_w_q", "ml_w_k",
          "ml_gate_bias", "ml_out_norm", "w_out", "norm_ffn", "router_group_w", "router_group_b",
          "router_expert_w", "router_expert_b", "moe_w_gate", "moe_w_up", "moe_w_down"]


def kernel(**inputs):
    import concourse.bacc as bacc
    from concourse.bass_utils import run_bass_kernel_spmd

    nc = bacc.Bacc("TRN2", target_bir_lowering=False, num_devices=1)
    arrays, aps = {}, {}
    consts = dict(zip(("consts", "onehot", "lncount"), shape_constants()))
    for name, value in [(n, inputs[n]) for n in INPUTS] + list(consts.items()):
        v = np.ascontiguousarray(value)
        arrays[f"in_{name}"] = v
        aps[name] = nc.dram_tensor(f"in_{name}", v.shape, mybir.dt.from_np(v.dtype), kind="ExternalInput").ap()
    out = nc.dram_tensor("out", (1, S, D), F32, kind="ExternalOutput").ap()
    build(nc, aps, aps["consts"], aps["onehot"], aps["lncount"], out)
    return run_bass_kernel_spmd(nc, [arrays], core_ids=[0]).results[0]["out"]
```

```python
from contextlib import ExitStack

import numpy as np

import concourse.bass as bass
from concourse import mybir

F32 = mybir.dt.float32
I32 = mybir.dt.int32
ALU = mybir.AluOpType
ACT = mybir.ActivationFunctionType
AX = mybir.AxisListType.X

P = 128
S = 256
NT = S // P
D = 2048
KT = D // P
DEPTH = 2
EPS = 1e-6
NEG = -1e30

H_A, QR, KVR, NOPE, ROPE, DV_A = 8, 384, 128, 64, 32, 64
QK_A = NOPE + ROPE
HALF = ROPE // 2
ROPE_THETA = 10000.0
H_D, HD_D = 12, 64
W_D = H_D * HD_D
PATTERNS = ((128, 1), (512, 4), (2048, 16))
N_BUCKETS, BUCKET_MAX = 32, 1024
H_M, HD_M, TAPS = 4, 192, 5
W_M = H_M * HD_M
CB = HD_M // 2
NCB = W_M // CB
NG, EPG, F_E = 4, 4, 512
NE = NG * EPG
CAP = 64
NE_PAD = NE + 2

C_IN = QR + KVR + ROPE + 3 * W_D + 3 * W_M + 4 * H_M
D_DQ = QR + KVR + ROPE
CQ, CKV = 0, QR
KR = QR + KVR
MG = KR + ROPE
DQ = MG + 4 * H_M
DK, DV = DQ + W_D, DQ + 2 * W_D
MU = DQ + 3 * W_D
MV, MO = MU + W_M, MU + 2 * W_M
CH = 256
SLOT = KT * CH
NSLOT = 6
N_MAIN = (C_IN - D_DQ - 4 * H_M) // CH
MAIN_ITERS = N_MAIN // NSLOT
N_OUT = D // CH

R_MIX, R_FFN = 0, KT
R_CQ = 2 * KT
R_CKV = R_CQ + QR // P
R_MLO = R_CKV + 1
R_DQ = R_MLO + W_M // P
R_DK = R_DQ + 1
N_ROW = R_DK + 1
R_CW, R_CB = 0, TAPS * NCB
R_AQ = R_CB + NCB
R_AK = R_AQ + 1
N_ROW96 = R_AK + 1
K_ID, K_FLIP, K_MASK = 0, P, 2 * P
K_FREQ = 3 * P
K_KEYG = K_FREQ + HALF
K_KEYE = K_KEYG + NG
N_CONST = K_KEYE + NE


def t5_buckets(rel):
    half = N_BUCKETS // 2
    exact = half // 2
    n = np.abs(rel)
    large = exact + (np.log(np.maximum(n, 1) / exact) / np.log(BUCKET_MAX / exact) * (half - exact)).astype(np.int32)
    large = np.minimum(large, half - 1)
    return (rel > 0).astype(np.int32) * half + np.where(n < exact, n, large).astype(np.int32)


def shape_constants():
    c = np.zeros((P, N_CONST), np.float32)
    c[:, K_ID:K_ID + P] = np.eye(P)
    c[:, K_FLIP:K_FLIP + P] = np.eye(P)[::-1]
    s, t = np.arange(P)[:, None], np.arange(P)[None, :]
    c[:, K_MASK:K_MASK + P] = np.where(s <= t, 0.0, NEG)
    c[:, K_FREQ:K_FREQ + HALF] = np.float32(ROPE_THETA) ** (-np.arange(HALF, dtype=np.float32) / np.float32(HALF))
    c[:, K_KEYG:K_KEYG + NG] = np.arange(NG, 0, -1)
    c[:, K_KEYE:K_KEYE + NE] = np.arange(NE, 0, -1)
    off = np.arange(2 * S) - (S - 1)
    onehot = np.zeros((N_BUCKETS, 2 * S), np.float32)
    onehot[t5_buckets(off), np.arange(2 * S)] = 1.0
    count = sum(((np.abs(off) <= w // 2) & (off % d == 0)).astype(np.int32) for w, d in PATTERNS)
    count[-1] = 0
    lncount = np.where(count > 0, np.log(np.maximum(count, 1)), NEG).astype(np.float32)
    return c, onehot, np.broadcast_to(lncount, (H_D, 2 * S)).copy()


class Uses:

    def __init__(self, n):
        self.n, self.at = n, {}
        self.count = {"pre": [0] * n, "layer": [0] * n, "post": [0] * n}
        self.part = "pre"

    def once(self, name, r):
        c = self.count[self.part]
        self.at[name] = (self.part, r, c[r], 0)
        c[r] += 1

    def loop(self, names, iters):
        c = self.count[self.part]
        per = [sum(r == q for _, r in names) for q in range(self.n)]
        seen = [0] * self.n
        for name, r in names:
            self.at[name] = (self.part, r, c[r] + seen[r], per[r])
            seen[r] += 1
        for q in range(self.n):
            c[q] += iters * per[q]

    def where(self, name):
        return self.at[name][1]

    def before(self, name, l=0, i=0):
        part, r, k, stride = self.at[name]
        if part == "pre":
            return k
        k += self.count["pre"][r]
        if part == "post":
            return k + DEPTH * self.count["layer"][r]
        return l * self.count["layer"][r] + k + (i * stride if stride else 0)


SCATTER_BANKS = (2, 3, 4, 5, 6, 7, 2, 3)


def plan_banks():
    b = Uses(8)
    for j in range(NT * KT // 4):
        b.once(f"x{j}", j % 8)
    for l in range(DEPTH):
        b.once(f"par{l}", 2 * l)
        b.once(f"par96{l}", 2 * l + 1)
    b.once("bias", 4)
    b.part = "layer"
    b.once("ssq", 0)
    for j in range(3):
        b.once(f"c{j}", 1 + j)
    for t in range(NT):
        b.once(f"lat{t}", 4 + t)
    for t in range(NT):
        for j in range(4):
            b.once(f"up{t}{j}", [6, 7, 0, 1, 2, 3, 4, 5][4 * t + j])
    b.loop([(f"m{j}", j) for j in range(NSLOT)], MAIN_ITERS - 1)
    plan_attention(b, "a", H_A, 1)
    for j in range(NSLOT):
        b.once(f"z{j}", j)
    for m in range(NCB // 2):
        b.once(f"mu{m}", (6, 7, 0, 1)[m])
    plan_attention(b, "d", H_D, 2)
    for d in range(2):
        b.once(f"rows{d}", d)
    b.once("gcols", 6)
    for h in range(H_M + 1):
        if h < H_M:
            b.once(f"mq{h}", 0)
            b.once(f"mk{h}", 1)
            b.once(f"w{h}0", 2)
            b.once(f"w{h}1", 3)
            b.once(f"ms{h}", 4 + h % 2)
        if h >= 1:
            b.once(f"n{h - 1}0", 6)
            b.once(f"n{h - 1}1", 7)
    for j in range(KT // 2):
        b.once(f"y{j}", j)
    for j in range(N_OUT):
        b.once(f"o{j}", j)
    b.once("ssq2", 0)
    for t in range(NT):
        b.once(f"route{t}", 1 + t)
    for j in range(NT * KT // 4):
        b.once(f"xt{j}", j)
    b.once("rank", 2)
    for n in range(4):
        b.once(f"gp{n}", 4 + n)
    body = [("g0", 0), ("u0", 1), ("g1", 2), ("ht0", 0)] + [(f"gx{n}", 4 + n) for n in range(4)]
    body += [("u1", 3), ("sw", 2), ("ht1", 1)] + [(f"dy{n}", 4 + n) for n in range(4)]
    body += [(f"sc{k}", SCATTER_BANKS[k]) for k in range(KT // 2)]
    b.loop(body, NE // 2)
    b.part = "post"
    for j in range(NT * KT // 4):
        b.once(f"f{j}", j % 8)
    return b


def plan_attention(b, k, heads, per):
    for s in range(heads + 3):
        if s < heads and s % per == 0:
            b.once(f"{k}t{s // per}", s // per % 2)
        if 1 <= s <= heads:
            b.once(f"{k}s{s - 1}", 2 + (s - 1) % 2)
        if 2 <= s <= heads + 1:
            b.once(f"{k}p{s - 2}", 4 + s % 2)
        if s >= 3:
            b.once(f"{k}o{s - 3}", 6 + (s - 3) % 2)


ONCE = [(f"c{j}", 1) for j in range(3)] + [("up", 1)]
MAIN = [(f"m{j}", MAIN_ITERS - 1) for j in range(NSLOT)]
THEN = [(f"z{j}", 1) for j in range(NSLOT)] + [("mw", 1)] + [(f"o{j}", 1) for j in range(N_OUT)]
EXPERT = [(f"{n}{j}", NE // 2) for n in ("g0", "u0", "g1", "u1", "dn0", "dn1") for j in range(2)]


def plan_slots():
    r = Uses(NSLOT)
    r.part = "layer"
    at = 0
    for group in (ONCE, MAIN, THEN, EXPERT):
        names = []
        for name, iters in group:
            names.append((name, at % NSLOT))
            at += 1
        if group in (MAIN, EXPERT):
            r.loop(names, group[0][1])
        else:
            for name, s in names:
                r.once(name, s)
    return r


BANKS, SLOTS = plan_banks(), plan_slots()
LAST_READER = {"up": "up13", "mw": f"mk{H_M - 1}"}
LAST_READER.update({f"{n}{j}": n for n in ("g0", "u0", "g1", "u1") for j in range(2)})
LAST_READER.update({f"dn{half}{j}": f"dy{2 * half + 1}" for half in range(2) for j in range(2)})


DVE_PRE, DVE_LAYER, ACT_LAYER = 18, 143, 20


class Steps:

    def __init__(self, eng, sem, pre, per_layer):
        self.eng, self.sem, self.pre, self.per_layer = eng, sem, pre, per_layer
        self.n, self.l, self.base = 0, None, 0

    def did(self, ins):
        ins.then_inc(self.sem, 1)
        self.n += 1

    def wait(self):
        self.eng.wait_ge(self.sem, self.n if self.l is None else self.base + self.n)

    def enter_layer(self, l):
        assert self.n == self.pre, f"pre {self.n}"
        self.l, self.n = l, 0
        self.base = l * self.per_layer + self.pre

    def enter_loop(self, i, per_turn):
        self.kept = (self.n, self.base, per_turn)
        self.base = self.base + self.n + i * per_turn
        self.n = 0

    def leave_loop(self, turns):
        n, base, per_turn = self.kept
        assert self.n == per_turn, f"turn {self.n}"
        self.n, self.base = n + turns * per_turn, base

    def leave_layer(self):
        assert self.n == self.per_layer, f"layer {self.n}"
        self.n, self.l = self.pre + DEPTH * self.per_layer, None


def build(nc, a, consts, onehot, lncount, out):
    with ExitStack() as ctx:
        def sb(name, shape, dt=F32):
            return ctx.enter_context(nc.sbuf_tensor(name, shape, dt))

        def sem(name):
            return ctx.enter_context(nc.semaphore(name))

        ring = sb("ring", [P, NSLOT, SLOT])
        X = sb("X", [P, KT, S])
        XN = sb("XN", [P, KT, S])
        PR = sb("PR", [P, NT, C_IN])
        BIAS = sb("BIAS", [P, H_D, S + P])
        K = sb("K", [P, N_CONST])
        scr = sb("scr", [P, 3 * 1024])
        v_mla = sb("v_mla", [P, NT, H_A * DV_A])
        ones = sb("ones", [P, P])
        par = sb("par", [P, DEPTH, N_ROW])
        par96 = sb("par96", [CB, DEPTH, N_ROW96])
        col, col96 = sb("col", [P, N_ROW]), sb("col96", [CB, N_ROW96])
        brow = sb("brow", [P, DEPTH, 4 * H_M + NG + NE])
        cs = sb("cs", [P, 2, NT, HALF])
        eps = sb("eps", [P, 1])
        std_x, rstd_x = sb("std_x", [P, NT]), sb("rstd_x", [P, NT])
        ss_lat, std_lat, rstd_lat = (sb(n, [P, 2, NT]) for n in ("ss_lat", "std_lat", "rstd_lat"))
        ss_a, rstd_a = sb("ss_a", [P, 2, NT, H_A]), sb("rstd_a", [P, 2, NT, H_A])
        ss_d, rstd_d = sb("ss_d", [P, 2, NT, H_D]), sb("rstd_d", [P, 2, NT, H_D])
        mx, nmx, psum_p = (sb(n, [P, 2, NT]) for n in ("mx", "nmx", "psum_p"))
        rs = sb("rs", [P, 4, NT])
        gcol = sb("gcol", [P, 2, 2, NT, H_M])
        std_d = sb("std_d", [P, 2, NT, H_D])
        std_a = sb("std_a", [P, 2, NT, H_A])
        std_m = sb("std_m", [P, H_M, NT])
        em = sb("em", [P, 2, NT, H_M])
        dn = sb("dn", [P, 2, 2, NT])
        ss_m, rstd_m = sb("ss_m", [P, H_M, NT]), sb("rstd_m", [P, H_M, NT])
        ps = ctx.enter_context(nc.psum_tensor("ps", [P, 8, 512], F32))
        sweep_load, sweep_pe, sweep_act, sweep_dve, sweep_own = map(
            sem, ("sweep_load", "sweep_pe", "sweep_act", "sweep_dve", "sweep_own"))
        bias_dram = nc.dram_tensor("bias_dram", (H_D, 2 * S), F32).ap()

        ident, flip = K[:, K_ID:K_ID + P], K[:, K_FLIP:K_FLIP + P]
        mask = K[:, K_MASK:K_MASK + P]
        prf = PR[:, :, :].rearrange("p t c -> p (t c)")
        SQ = prf[:, 0:KT * S].rearrange("p (k s) -> p k s", k=KT)
        xtok = prf[:, 0:NT * D].rearrange("p (t d) -> p t d", t=NT)
        at = KT * S
        tri = prf[:, at:at + P]
        Sw = prf[0:2 * CAP, at + P:at + P + S]
        routed = prf[:, at + 384:at + 384 + 3 * NT * NE_PAD]
        rank, picked, comb = (routed[:, n * NT * NE_PAD:(n + 1) * NT * NE_PAD].rearrange("p (t e) -> p t e", t=NT) for n in range(3))
        iota = prf[:, at + 512:at + 512 + CAP]
        combB = prf[:, at:at + NE * S].rearrange("p (e s) -> p e s", e=NE)
        Y = prf[0:2 * CAP, 8192:8192 + D]
        comb2 = prf[:, 10240:10240 + NT * NE].rearrange("p (t e) -> p t e", t=NT)
        q_mla, k_mla = PR[:, :, MV:MV + W_M], PR[:, :, MO:MO + W_M]
        qkT = scr[:, 0:1024].rearrange("p (b n) -> p b n", b=2)
        prob = scr[:, 1024:2048].rearrange("p (b t n) -> p b t n", b=2, t=NT)
        pT = scr[:, 2048:3072].rearrange("p (b t n) -> p b t n", b=2, t=NT)
        latT = scr[:, 2048:3072].rearrange("p (k s) -> p k s", s=S)
        rtmp = scr[:, 1024:2048].rearrange("p (a t h n) -> p a t h n", a=4, t=NT, h=H_A)
        decay = scr[:, 0:4 * 3 * P].rearrange("p (b d n) -> p b d n", b=2, d=2)
        hT = scr[:, 0:4 * S].rearrange("p (k n) -> p k n", k=4)
        ang = scr[:, 0:4 * NT * HALF].rearrange("p (a t n) -> p a t n", a=4, t=NT)
        pos_i, pos_f = scr[:, 128:128 + NT].bitcast(I32), scr[:, 128 + NT:128 + 2 * NT]
        rt = scr[:, 1792:1792 + 6 * NT * NE].rearrange("p (a t n) -> p a t n", a=6, t=NT)
        lg = scr[:, 1984:1984 + NT * (NG + NE)].rearrange("p (t n) -> p t n", t=NT)
        fl = sb("fl", [P, 2])
        fi = sb("fi", [P, 2], I32)
        rs1 = scr[:, 2024:2040].rearrange("p (a t) -> p a t", t=NT)
        w_rt = scr[:, 2048:2048 + KT * (NG + NE)].rearrange("p (k n) -> p k n", k=KT)
        combT = scr[0:NE, 1536:1536 + S]
        vf = v_mla[:, :, :].rearrange("p t n -> p (t n)")
        hs = scr[:, 0:8 * CAP].rearrange("p (k n) -> p k n", k=4)
        sgs = scr[0:2 * CAP, 512:512 + F_E]
        XG = scr[:, 1024:1024 + KT * 2 * CAP].rearrange("p (k n) -> p k n", k=KT)
        gated = vf[0:2 * CAP, 0:F_E]
        Gm = vf[:, 512:512 + 4 * CAP].rearrange("p (t n) -> p t n", t=NT)
        Gw = vf[:, 768:768 + 4 * CAP].rearrange("p (t n) -> p t n", t=NT)
        sg = scr[:, 2048:3072].rearrange("p (b n) -> p b n", b=2)
        xnf = XN[:, :, :].rearrange("p k s -> p (k s)")
        uc = xnf[0:CB, 0:NCB * S].rearrange("p (b s) -> p b s", b=NCB)
        u_raw = xnf[0:CB, NCB * S:2 * NCB * S].rearrange("p (b s) -> p b s", b=NCB)
        mqk = xnf[0:CB, NCB * S:2 * NCB * S].rearrange("p (b q n) -> p b q n", b=2, q=2)
        raw = xnf[0:N_ROW, 0:DEPTH * P].rearrange("p (l n) -> p l n", l=DEPTH)
        raw96 = xnf[0:N_ROW96, 512:512 + DEPTH * CB].rearrange("p (l n) -> p l n", l=DEPTH)
        oh = xnf[0:N_BUCKETS, 1024:1024 + 2 * S]
        rb = xnf[0:N_BUCKETS, 1536:1536 + H_D]
        lnc = xnf[0:H_D, 2048:2048 + 2 * S]
        fbias = scr[0:H_D, 512:512 + 2 * S]

        def grow(d, j):
            return PR[0:H_M, d, DK + j * S:DK + (j + 1) * S]

        slot_full = [sem(f"slot_full{s}") for s in range(NSLOT)]
        psum_full = [sem(f"psum_full{b}") for b in range(8)]
        psum_free = [sem(f"psum_free{b}") for b in range(8)]
        dve_steps, act_steps = sem("dve_steps"), sem("act_steps")
        gains_in, rows_in = [sem("gains_in_pool"), sem("gains_in_sp")], sem("rows_in")
        x_in, const_in, bias_in, bias_out, pos_in, rw_in, done = map(
            sem, ("x_in", "const_in", "bias_in", "bias_out", "pos_in", "rw_in", "done"))
        c2_full, up_full, mw_full = sem("c2_full"), sem("up_full"), sem("mw_full")
        ones_set, ang_set = sem("ones_set"), sem("ang_set")

        stages = {}

        def stage(name, n=1):
            stages[name] = (sem(name), n)

        def signal(name):
            return stages[name][0], 1

        def after(name, l, j=0, i=None, stride=0):
            s, n = stages[name]
            return s, l * n + (j + 1) + (0 if i is None else i * stride)

        for name, n in (("cols", 2), ("sq", 4), ("xg", KT), ("rstd_x", 1), ("lat_std", 1), ("lat_n", 1),
                        ("a_roped", 1), ("a_sq", 1), ("a_ss", 1), ("a_std", 1), ("a_n", 1),
                        ("d_sq", 1), ("d_ss", 1), ("d_std", 1), ("d_n", 1), ("nmax", H_A + H_D), ("rsum", H_A + H_D),
                        ("gate_b", 1), ("gate_ln", 2), ("rows_ready", 2), ("em_ready", 1), ("conv", NCB // 2), ("uc_ready", H_M),
                        ("r_ready", H_M), ("m_std", 1), ("y_ml", 1), ("sq2", 4), ("xn2", KT),
                        ("e_in", 2), ("e_exp", 2), ("picked", 1), ("flags", 1), ("gm", 1 + NE // 2), ("gw", NE // 2)):
            stage(name, n)

        def bank(name):
            return ps[:, BANKS.where(name), :]

        def ready(name, l=0, i=0):
            return psum_full[BANKS.where(name)], BANKS.before(name, l, i) + 1

        def freed(name, l=0, i=0):
            return psum_free[BANKS.where(name)], BANKS.before(name, l, i)

        def copied(name, l=0, i=0):
            return psum_free[BANKS.where(name)], BANKS.before(name, l, i) + 1

        def made(name):
            return psum_full[BANKS.where(name)], 1

        def read(name):
            return psum_free[BANKS.where(name)], 1

        def slot(name):
            return ring[:, SLOTS.where(name), :]

        def empty(name, l, turn=0):
            pair = [n for n, _ in EXPERT]
            at = pair.index(name) if name in pair else None
            if at is not None and at >= NSLOT:
                return ready(LAST_READER[pair[at - NSLOT]], l, turn)
            if not (isinstance(turn, int) and turn == 0):
                return ready(name if at is None else LAST_READER[pair[at + NSLOT]], l, turn - 1)
            s = SLOTS.where(name)
            order = [n for n, _ in ONCE + MAIN + THEN + EXPERT if SLOTS.where(n) == s]
            before = order[order.index(name) - 1]
            turns = dict(ONCE + MAIN + THEN + EXPERT)[before]
            if order.index(name) > 0:
                return ready(LAST_READER.get(before, before), l, turns - 1)
            assert DEPTH == 2
            bank_full, value = ready(LAST_READER.get(before, before), 0, turns - 1)
            return bank_full, l * (value - 1) + 1

        skip = {}
        for n in ("c2", "up", "mw"):
            skip.setdefault(SLOTS.where(n), []).append(SLOTS.at[n][2])

        def loaded(name, l, i=0):
            s = SLOTS.where(name)
            k, stride = SLOTS.at[name][2:]
            own = skip.get(s, [])
            k -= sum(o < k for o in own)
            n = SLOTS.count["layer"][s] - len(own)
            return slot_full[s], 16 * (l * n + (k + 1) + (i * stride if stride else 0))

        def heads(t, off, n, w):
            return PR[:, t, off:off + n * w].rearrange("p (h w) -> p h w", h=n)

        SWEEP_DVE, SWEEP_PE = 3 + 2 * NE, 2 + 3 * NE
        SWEEP_BLOCKS = [(w, half) for half in range(2) for w in ("moe_w_gate", "moe_w_up")] + [("moe_w_down", half) for half in range(2)]

        def wait_alone(eng, semaphore, value):
            value = eng.to_reg(value)
            eng.wait_ge(ones_set, 2)
            eng.wait_ge(semaphore, value)

        def sweep_due(eng):
            return (eng.value_load(fi[0:1, 1:2], min_val=0, max_val=DEPTH), eng.value_load(fi[0:1, 0:1], min_val=0, max_val=1))

        block = ctx.enter_context(nc.Block())

        def load_gains(eng, l, arrived):
            r = raw[:, l, :]
            for at, n, src in ((R_MIX, KT, a["norm_mix"][l]), (R_FFN, KT, a["norm_ffn"][l]),
                               (R_CQ, 3, a["mla_norm_cq"][l]), (R_CKV, 1, a["mla_norm_ckv"][l]),
                               (R_MLO, 6, a["ml_out_norm"][l])):
                eng.dma_start(r[at:at + n, :], src.rearrange("(r c) -> r c", c=P)).then_inc(arrived, 16)
            for at, src in ((R_DQ, a["dil_q_norm"][l]), (R_DK, a["dil_k_norm"][l])):
                for h in range(2):
                    eng.dma_start(r[at:at + 1, h * HD_D:(h + 1) * HD_D], src.unsqueeze(0)).then_inc(arrived, 16)

        def load_rows96(eng, l, arrived):
            r = raw96[:, l, :]
            eng.dma_start(r[R_CW:R_CW + TAPS * NCB, :], a["ml_conv_w"][l].rearrange("t (b c) -> (t b) c", c=CB)).then_inc(arrived, 16)
            eng.dma_start(r[R_CB:R_CB + NCB, :], a["ml_conv_b"][l].rearrange("(b c) -> b c", c=CB)).then_inc(arrived, 16)
            eng.dma_start(r[R_AQ:R_AQ + 1, :], a["mla_q_norm"][l].unsqueeze(0)).then_inc(arrived, 16)
            eng.dma_start(r[R_AK:R_AK + 1, :], a["mla_k_norm"][l].unsqueeze(0)).then_inc(arrived, 16)

        def load_biases(eng, l, arrived):
            for at, n, src in ((0, 4 * H_M, a["ml_gate_bias"][l].rearrange("d i h -> (d i h)")),
                               (4 * H_M, NG, a["router_group_b"][l]), (4 * H_M + NG, NE, a["router_expert_b"][l])):
                eng.dma_start(brow[:, l, at:at + n], src.partition_broadcast(P)).then_inc(arrived, 16)

        @block.sync
        def _(sp):
            for t in range(NT):
                sp.dma_start(PR[:, t, 0:D], a["x"][0, t * P:(t + 1) * P, :]).then_inc(x_in, 16)
            for l in range(1, DEPTH):
                load_gains(sp, l, gains_in[1])

            def w_cols(l, lo, n):
                return a["w_in"][l, :, lo:lo + n].rearrange("(k p) c -> p k c", p=P)

            def load(name, l, src, turn=0, k=KT):
                sp.wait_ge(*empty(name, l, turn))
                sp.dma_start(slot(name).rearrange("p (k c) -> p k c", k=k), src).then_inc(
                    slot_full[SLOTS.where(name)], 16)

            with sp.Fori(0, DEPTH) as l:
                for j in range(2):
                    load(f"c{j}", l, w_cols(l, j * CH, CH))
                sp.wait_ge(*empty("c2", l))
                nar = slot("c2")[:, 0:KT * 48].rearrange("p (k c) -> p k c", k=KT)
                sp.dma_start(nar[:, :, 0:ROPE], w_cols(l, KR, ROPE)).then_inc(c2_full, 16)
                sp.dma_start(nar[:, :, ROPE:48], w_cols(l, C_IN - 4 * H_M, 4 * H_M)).then_inc(c2_full, 16)
                sp.wait_ge(*empty("up", l))
                sp.dma_start(slot("up")[:, 0:3 * W_D].rearrange("p (k c) -> p k c", k=3),
                             a["mla_w_uq"][l].rearrange("(k p) c -> p k c", p=P)).then_inc(up_full, 16)
                sp.dma_start(slot("up")[:, 3 * W_D:3 * W_D + 1024], a["mla_w_ukv"][l]).then_inc(up_full, 16)
                for i in range(MAIN_ITERS - 1):
                    for j in range(NSLOT):
                        load(f"m{j}", l, w_cols(l, D_DQ + (i * NSLOT + j) * CH, CH), i)
                for j in range(NSLOT):
                    load(f"z{j}", l, w_cols(l, D_DQ + ((MAIN_ITERS - 1) * NSLOT + j) * CH, CH))
                sp.wait_ge(*empty("mw", l))
                for n, w in enumerate(("ml_w_q", "ml_w_k")):
                    sp.dma_start(slot("mw")[0:CB, n * NCB * HD_M:(n + 1) * NCB * HD_M].rearrange("p (b e) -> p b e", b=NCB),
                                 a[w][l].rearrange("h (b p) e -> p (h b) e", p=CB)).then_inc(mw_full, 16)
                for j in range(N_OUT):
                    load(f"o{j}", l, a["w_out"][l, :, j * CH:(j + 1) * CH].rearrange("(k p) c -> p k c", p=P))
                sp.wait_ge(*after("y_ml", l))
                sp.dma_start(w_rt[:, :, 0:NG], a["router_group_w"][l].rearrange("(k p) c -> p k c", p=P)).then_inc(rw_in, 16)
                sp.dma_start(w_rt[:, :, NG:], a["router_expert_w"][l].rearrange("(k p) c -> p k c", p=P)).then_inc(rw_in, 16)

                def half_of(w, e, half):
                    if w == "moe_w_down":
                        return a[w][l].rearrange("e (k p) c -> e p k c", p=P)[
                            bass.ds(e, 1), :, :, half * 1024:(half + 1) * 1024].rearrange("e p k c -> (e p) k c")
                    return a[w][l].rearrange("e (k p) f -> e p k f", p=P)[
                        bass.ds(e, 1), :, :, half * CH:(half + 1) * CH].rearrange("e p k f -> (e p) k f")

                def load_pair(i):
                    for half in range(2):
                        for n, w in (("g", "moe_w_gate"), ("u", "moe_w_up")):
                            for j in range(2):
                                load(f"{n}{half}{j}", l, half_of(w, 2 * i + j, half), i)
                    for half in range(2):
                        for j in range(2):
                            load(f"dn{half}{j}", l, half_of("moe_w_down", 2 * i + j, half), i, k=4)

                load_pair(0)
                with sp.Fori(1, NE // 2) as i:
                    load_pair(i)
                wait_alone(sp, *after("flags", l))
                runs, due = sweep_due(sp)
                with sp.If(due > 0):
                    with sp.Fori(0, NE) as e:
                        sp.wait_ge(sweep_dve, runs * SWEEP_DVE + 3 + e * 2)
                        for n, (w, half) in enumerate(SWEEP_BLOCKS):
                            sp.dma_start(ring[:, n, :].rearrange("p (k c) -> p k c", k=4 if w == "moe_w_down" else KT),
                                         half_of(w, e, half)).then_inc(sweep_load, 16)
                    wait_alone(sp, sweep_dve, runs * SWEEP_DVE + SWEEP_DVE)
            for t in range(NT):
                for g in range(KT // 4):
                    sp.wait_ge(*copied(f"f{t * KT // 4 + g}"))
                sp.dma_start(out[0, t * P:(t + 1) * P, :], PR[:, t, 0:D]).then_inc(done, 16)
            sp.wait_ge(done, 16 * NT)

        @block.gpsimd
        def _(pool):
            pool.dma_start(K[:, :], consts).then_inc(const_in, 16)
            load_gains(pool, 0, gains_in[0])
            pool.dma_start(oh, onehot).then_inc(bias_in, 16)
            pool.dma_start(lnc, lncount).then_inc(bias_in, 16)
            pool.dma_start(rb, a["rel_bias"]).then_inc(bias_in, 16)
            pool.dma_start(pos_i[:, :], a["positions"][0].rearrange("(t p) -> p t", p=P),
                           allow_slow_non_contiguous=True).then_inc(pos_in, 16)
            pool.wait_ge(*copied("bias"))
            pool.dma_start(bias_dram, fbias).then_inc(bias_out, 16)
            pool.wait_ge(bias_out, 16)
            pool.dma_start(BIAS[:, :, :], bass.AP(bias_dram.tensor, 0, [[1, P], [2 * S, H_D], [1, S + P]])).then_inc(bias_out, 16)
            pool.wait_ge(bias_out, 32)

        def wait_parameters(eng):
            eng.wait_ge(gains_in[0], 16 * (5 + 4))
            eng.wait_ge(gains_in[1], 16 * (5 + 4) * (DEPTH - 1))
            eng.wait_ge(rows_in, 16 * (4 + 3) * DEPTH)

        @block.tensor
        def _(pe):
            def mm(o, lhsT, rhs, start=True, stop=True):
                return pe.matmul(o, lhsT, rhs, start=start, stop=stop, skip_group_check=True)

            pe.wait_ge(const_in, 16)
            pe.wait_ge(ones_set, 2)
            for t in range(NT):
                pe.wait_ge(x_in, 16 * (t + 1))
                if t == 0:
                    pe.wait_ge(x_in, 16 * NT)
                for g in range(KT // 4):
                    name = f"x{t * KT // 4 + g}"
                    pe.wait_ge(*freed(name))
                    for q in range(4):
                        last = pe.transpose(bank(name)[:, q * P:(q + 1) * P], PR[:, t, (4 * g + q) * P:(4 * g + q + 1) * P], ident)
                    last.then_inc(*made(name))
            wait_parameters(pe)
            for l in range(DEPTH):
                pe.wait_ge(*freed(f"par{l}"))
                pe.transpose(bank(f"par{l}")[:, 0:N_ROW], raw[:, l, :], K[0:N_ROW, K_ID:K_ID + N_ROW]).then_inc(*made(f"par{l}"))
                pe.wait_ge(*freed(f"par96{l}"))
                pe.transpose(bank(f"par96{l}")[0:CB, 0:N_ROW96], raw96[:, l, :], K[0:N_ROW96, K_ID:K_ID + N_ROW96]).then_inc(*made(f"par96{l}"))
            pe.wait_ge(bias_in, 48)
            pe.wait_ge(*freed("bias"))
            mm(bank("bias")[0:H_D, :], rb, oh).then_inc(*made("bias"))

            def project(name, sname, l, w, i=0):
                pe.wait_ge(*freed(name, l, i))
                for t in range(NT):
                    for k in range(KT):
                        if name == "c0" and t == 0:
                            pe.wait_ge(*after("xg", l, k))
                        last = mm(bank(name)[:, t * CH:t * CH + w.shape[2]], XN[:, k, t * P:(t + 1) * P], w[:, k, :],
                                  k == 0, k == KT - 1)
                last.then_inc(*made(name))

            def attention(kind, n_heads, per, l):
                for s in range(n_heads + 3):
                    if s < n_heads and s % per == 0:
                        u = s // per
                        name = f"{kind}t{u}"
                        pe.wait_ge(*freed(name, l))
                        for n in range(2):
                            for t in range(NT):
                                if kind == "a":
                                    src = (q_mla, k_mla)[n][:, t, u * QK_A:(u + 1) * QK_A]
                                    o = bank(name)[0:QK_A, (2 * n + t) * P:(2 * n + t + 1) * P]
                                else:
                                    src = PR[:, t, (DQ, DK)[n] + u * P:(DQ, DK)[n] + (u + 1) * P]
                                    o = bank(name)[:, (2 * n + t) * P:(2 * n + t + 1) * P]
                                last = pe.transpose(o, src, ident)
                        last.then_inc(*made(name))
                    if 1 <= s <= n_heads:
                        h = s - 1
                        name = f"{kind}s{h}"
                        lo, kd = (0, QK_A) if kind == "a" else (HD_D * (h % 2), HD_D)
                        qk = qkT[lo:lo + kd, h // per % 2, :]
                        pe.wait_ge(*freed(name, l))
                        pe.wait_ge(*copied(f"{kind}t{h // per}", l))
                        for t in range(NT):
                            o = bank(name)[:, t * S:(t + 1) * S]
                            if kind == "d":
                                mm(o, flip, BIAS[:, h, P - t * P:P - t * P + S], True, False)
                            last = mm(o, qk[:, t * P:(t + 1) * P], qk[:, S:2 * S], kind == "a", True)
                        last.then_inc(*made(name))
                    if 2 <= s <= n_heads + 1:
                        h = s - 2
                        name = f"{kind}p{h}"
                        pe.wait_ge(*freed(name, l))
                        pe.wait_ge(*copied(f"{kind}s{h}", l))
                        for kt in range(NT):
                            for t in range(NT):
                                last = pe.transpose(bank(name)[:, (kt * NT + t) * P:(kt * NT + t + 1) * P],
                                                    prob[:, h % 2, t, kt * P:(kt + 1) * P], ident)
                        last.then_inc(*made(name))
                    if s >= 3:
                        h = s - 3
                        name = f"{kind}o{h}"
                        pe.wait_ge(*freed(name, l))
                        pe.wait_ge(*copied(f"{kind}p{h}", l))
                        for t in range(NT):
                            for kt in range(NT):
                                v = v_mla[:, kt, h * DV_A:(h + 1) * DV_A] if kind == "a" else PR[:, kt, DV + h * HD_D:DV + (h + 1) * HD_D]
                                last = mm(bank(name)[:, t * 64:(t + 1) * 64], pT[:, h % 2, kt, t * P:(t + 1) * P], v,
                                          kt == 0, kt == NT - 1)
                        last.then_inc(*made(name))

            with pe.Fori(0, DEPTH) as l:
                pe.wait_ge(*freed("ssq", l))
                pe.wait_ge(*after("sq", l, 3))
                for t in range(NT):
                    for k in range(KT):
                        last = mm(bank("ssq")[:, t:t + 1], SQ[:, k, t * P:(t + 1) * P], ones[:, 0:1], k == 0, k == KT - 1)
                last.then_inc(*made("ssq"))
                for j in range(3):
                    w = slot(f"c{j}")
                    if j < 2:
                        pe.wait_ge(*loaded(f"c{j}", l))
                        project(f"c{j}", f"c{j}", l, w.rearrange("p (k c) -> p k c", k=KT))
                    else:
                        pe.wait_ge(c2_full, (l + 1) * 32)
                        project("c2", "c2", l, w[:, 0:KT * 48].rearrange("p (k c) -> p k c", k=KT))
                pe.wait_ge(*after("lat_n", l))
                for t in range(NT):
                    pe.wait_ge(*freed(f"lat{t}", l))
                    for k in range(4):
                        last = pe.transpose(bank(f"lat{t}")[:, k * P:(k + 1) * P], PR[:, t, k * P:(k + 1) * P], ident)
                    last.then_inc(*made(f"lat{t}"))
                pe.wait_ge(up_full, (l + 1) * 32)
                pe.wait_ge(*copied("lat1", l))
                for t in range(NT):
                    for j in range(4):
                        name = f"up{t}{j}"
                        pe.wait_ge(*freed(name, l))
                        if j < 2:
                            for k in range(3):
                                last = mm(bank(name)[:, 0:384], latT[:, k, t * P:(t + 1) * P],
                                          slot("up")[:, k * W_D + j * 384:k * W_D + (j + 1) * 384], k == 0, k == 2)
                        else:
                            last = mm(bank(name), latT[:, 3, t * P:(t + 1) * P],
                                      slot("up")[:, 3 * W_D + (j - 2) * 512:3 * W_D + (j - 1) * 512])
                        last.then_inc(*made(name))
                with pe.Fori(0, MAIN_ITERS - 1) as i:
                    for j in range(NSLOT):
                        pe.wait_ge(*loaded(f"m{j}", l, i))
                        project(f"m{j}", f"m{j}", l, slot(f"m{j}").rearrange("p (k c) -> p k c", k=KT), i)
                pe.wait_ge(*after("a_n", l))
                attention("a", H_A, 1, l)
                for j in range(NSLOT):
                    pe.wait_ge(*loaded(f"z{j}", l))
                    project(f"z{j}", f"z{j}", l, slot(f"z{j}").rearrange("p (k c) -> p k c", k=KT))
                for j in range(NSLOT):
                    pe.wait_ge(*copied(f"z{j}", l))
                for m in range(NCB // 2):
                    name = f"mu{m}"
                    pe.wait_ge(*freed(name, l))
                    for b in range(2):
                        for t in range(NT):
                            c = MU + (2 * m + b) * CB
                            last = pe.transpose(bank(name)[0:CB, b * S + t * P:b * S + (t + 1) * P], PR[:, t, c:c + CB], ident)
                    last.then_inc(*made(name))
                pe.wait_ge(*after("d_n", l))
                pe.wait_ge(bias_out, 32)
                attention("d", H_D, 2, l)

                pe.wait_ge(*after("gate_b", l))
                for d in range(2):
                    pe.wait_ge(*freed(f"rows{d}", l))
                    for n in range(2):
                        for t in range(NT):
                            g = MG + (2 * d + n) * H_M
                            last = mm(bank(f"rows{d}")[0:H_M, n * S + t * P:n * S + (t + 1) * P], PR[:, t, g:g + H_M], ident)
                    last.then_inc(*made(f"rows{d}"))
                pe.wait_ge(*freed("gcols", l))
                for d in range(2):
                    pe.wait_ge(*after("rows_ready", l, d))
                    for n in range(2):
                        for t in range(NT):
                            c = ((n * 2 + d) * NT + t) * H_M
                            last = mm(bank("gcols")[:, c:c + H_M], grow(d, (2, 4)[n])[:, t * P:(t + 1) * P], K[0:H_M, 0:H_M])
                last.then_inc(*made("gcols"))
                pe.wait_ge(mw_full, (l + 1) * 32)
                for h in range(H_M + 1):
                    if h < H_M:
                        for n, c in enumerate("qk"):
                            name = f"m{c}{h}"
                            pe.wait_ge(*freed(name, l))
                            if n == 0:
                                pe.wait_ge(*after("uc_ready", l, h))
                            for e in range(2):
                                for b in range(2):
                                    w = (n * NCB + 2 * h + b) * HD_M + e * CB
                                    last = mm(bank(name)[0:CB, e * S:(e + 1) * S], slot("mw")[0:CB, w:w + CB],
                                              uc[:, 2 * h + b, :], b == 0, b == 1)
                            last.then_inc(*made(name))
                        for d in range(2):
                            name = f"w{h}{d}"
                            pe.wait_ge(*freed(name, l))
                            pick = K[0:H_M, h:h + 1].to_broadcast([H_M, P])
                            neg_m = grow(d, 0)
                            o = bank(name)
                            if d == 0:
                                mm(o[:, 0:S], pick, neg_m, True, False)
                                mm(o[:, 0:P], ident, mask, False, True)
                                mm(o[:, S:S + P], pick, neg_m[:, P:S], True, False)
                                last = mm(o[:, S:S + P], ident, mask, False, True)
                            else:
                                mm(o[:, 0:P], pick, neg_m[:, 0:P], True, False)
                                mm(o[:, 0:P], mask, ident, False, True)
                                mm(o[:, P:P + S], pick, neg_m, True, False)
                                last = mm(o[:, S:S + P], mask, ident, False, True)
                            last.then_inc(*made(name))
                        name = f"ms{h}"
                        pe.wait_ge(*freed(name, l))
                        pe.wait_ge(*copied(f"mq{h}", l))
                        pe.wait_ge(*copied(f"mk{h}", l))
                        for s in range(NT):
                            for e in range(2):
                                last = mm(bank(name)[:, s * S:(s + 1) * S], mqk[:, h % 2, 1, e * S + s * P:e * S + (s + 1) * P],
                                          mqk[:, h % 2, 0, e * S:(e + 1) * S], e == 0, e == 1)
                        last.then_inc(*made(name))
                    if h >= 1:
                        g = h - 1
                        pe.wait_ge(*copied(f"ms{g}", l))
                        for d in range(2):
                            name = f"n{g}{d}"
                            pe.wait_ge(*freed(name, l))
                            of = ((0, ((0, 0),)), (1, ((1, 0), (2, 1)))) if d == 0 else ((0, ((0, 0), (1, 1))), (1, ((2, 1),)))
                            for t, parts in of:
                                for lo, n, src in ((0, HD_M, "v"), (HD_M, 1, "1")):
                                    for j, (blk, s) in enumerate(parts):
                                        rhs = PR[:, s, MV + g * HD_M:MV + (g + 1) * HD_M] if src == "v" else ones[:, 0:1]
                                        last = mm(bank(name)[:, t * S + lo:t * S + lo + n],
                                                  decay[:, g % 2, d, blk * P:(blk + 1) * P], rhs,
                                                  j == 0, j == len(parts) - 1)
                            last.then_inc(*made(name))
                for j in range(KT // 2):
                    name = f"y{j}"
                    pe.wait_ge(*freed(name, l))
                    if j == 0:
                        pe.wait_ge(*copied(f"do{H_D - 1}", l))
                    if j == 5:
                        pe.wait_ge(*after("y_ml", l))
                    for q in range(2):
                        kk = 2 * j + q
                        c = kk * P if kk < 4 else DQ + (kk - 4) * P if kk < 10 else MU + (kk - 10) * P
                        for t in range(NT):
                            last = pe.transpose(bank(name)[:, q * S + t * P:q * S + (t + 1) * P], PR[:, t, c:c + P], ident)
                    last.then_inc(*made(name))
                for j in range(N_OUT):
                    name = f"o{j}"
                    w = slot(name).rearrange("p (k c) -> p k c", k=KT)
                    pe.wait_ge(*loaded(name, l))
                    pe.wait_ge(*freed(name, l))
                    if j == 0:
                        for q in (KT // 2 - 2, KT // 2 - 1):
                            pe.wait_ge(*copied(f"y{q}", l))
                    for q in range(2):
                        for k in range(KT):
                            last = mm(bank(name)[:, q * S:(q + 1) * S], w[:, k, q * P:(q + 1) * P], XN[:, k, :], k == 0, k == KT - 1)
                    last.then_inc(*made(name))
                pe.wait_ge(*freed("ssq2", l))
                for k in range(KT):
                    if k % 4 == 0:
                        pe.wait_ge(*after("sq2", l, k // 4))
                    last = mm(bank("ssq2")[:, 0:S], ones[:, 0:P], SQ[:, k, :], k == 0, k == KT - 1)
                last.then_inc(*made("ssq2"))
                for t in range(NT):
                    pe.wait_ge(*freed(f"route{t}", l))
                pe.wait_ge(rw_in, (l + 1) * 32)
                for k in range(KT):
                    pe.wait_ge(*after("xn2", l, k))
                    for t in range(NT):
                        last = mm(bank(f"route{t}")[:, 0:NG + NE], XN[:, k, t * P:(t + 1) * P], w_rt[:, k, :], k == 0, k == KT - 1)
                        if k == KT - 1:
                            last.then_inc(*made(f"route{t}"))
                for j in range(NT * KT // 4):
                    t, g = j // (KT // 4), j % (KT // 4)
                    pe.wait_ge(*freed(f"xt{j}", l))
                    for q in range(4):
                        last = pe.transpose(bank(f"xt{j}")[:, q * P:(q + 1) * P], XN[:, 4 * g + q, t * P:(t + 1) * P], ident)
                    last.then_inc(*made(f"xt{j}"))
                pe.wait_ge(*freed("rank", l))
                pe.wait_ge(*after("picked", l))
                o = bank("rank")
                mm(o[:, 0:NE], tri, picked[:, 0, 0:NE])
                mm(o[:, NE:2 * NE], ones[:, :], picked[:, 0, 0:NE], True, False)
                mm(o[:, NE:2 * NE], tri, picked[:, 1, 0:NE], False, True)
                mm(o[:, 2 * NE:3 * NE], ones[:, :], picked[:, 0, 0:NE], True, False)
                mm(o[:, 2 * NE:3 * NE], ones[:, :], picked[:, 1, 0:NE], False, True).then_inc(*made("rank"))

                def gather(kind, i=0):
                    for n in range(4):
                        name = f"{kind}{n}"
                        pe.wait_ge(*freed(name, l, i))
                        for k in range(4):
                            d = (4 * n + k) * P
                            for t in range(NT):
                                last = mm(bank(name)[:, k * 2 * CAP:(k + 1) * 2 * CAP], xtok[:, t, d:d + P], Gm[:, t, :], t == 0, t == NT - 1)
                        last.then_inc(*made(name))

                for j in (NT * KT // 4 - 2, NT * KT // 4 - 1):
                    pe.wait_ge(*copied(f"xt{j}", l))
                pe.wait_ge(*after("gm", l, 0))
                gather("gp")
                with pe.Fori(0, NE // 2) as i:
                    def project(name):
                        w = [slot(f"{name}{j}").rearrange("p (k c) -> p k c", k=KT) for j in range(2)]
                        for j in range(2):
                            pe.wait_ge(*loaded(f"{name}{j}", l, i))
                        pe.wait_ge(*freed(name, l, i))
                        for k in range(KT):
                            for j in range(2):
                                own_rows = slice(j * CAP, (j + 1) * CAP)
                                last = mm(bank(name)[own_rows, 0:CH], XG[:, k, own_rows], w[j][:, k, :], k == 0, k == KT - 1)
                        last.then_inc(*made(name))

                    def turn_h(half):
                        name = f"ht{half}"
                        pe.wait_ge(*copied(f"u{half}", l, i))
                        pe.wait_ge(*freed(name, l, i))
                        for q in range(2):
                            last = pe.transpose(bank(name)[:, q * 2 * CAP:(q + 1) * 2 * CAP], gated[:, (2 * half + q) * P:(2 * half + q + 1) * P], ident)
                        last.then_inc(*made(name))

                    for n in range(4):
                        pe.wait_ge(*freed(f"gx{n}", l, i))
                    project("g0")
                    project("u0")
                    project("g1")
                    turn_h(0)
                    pe.wait_ge(*after("gm", l, 1, i, 1))
                    gather("gx", i)
                    project("u1")
                    pe.wait_ge(*freed("sw", l, i))
                    pe.wait_ge(*after("gw", l, 0, i, 1))
                    for t in range(NT):
                        last = pe.transpose(bank("sw")[0:2 * CAP, t * P:(t + 1) * P], Gw[:, t, :], ident)
                    last.then_inc(*made("sw"))
                    turn_h(1)
                    for half in range(2):
                        pe.wait_ge(*copied(f"ht{half}", l, i))
                    for half in range(2):
                        w = [slot(f"dn{half}{j}").rearrange("p (k c) -> p k c", k=4) for j in range(2)]
                        for j in range(2):
                            pe.wait_ge(*loaded(f"dn{half}{j}", l, i))
                        for q in range(2):
                            name = f"dy{2 * half + q}"
                            pe.wait_ge(*freed(name, l, i))
                            for k in range(4):
                                for j in range(2):
                                    own_rows = slice(j * CAP, (j + 1) * CAP)
                                    last = mm(bank(name)[own_rows, :], hs[:, k, own_rows], w[j][:, k, q * 512:(q + 1) * 512], k == 0, k == 3)
                            last.then_inc(*made(name))
                    pe.wait_ge(*copied("sw", l, i))
                    for n in range(4):
                        pe.wait_ge(*copied(f"dy{n}", l, i))
                    for k in range(KT // 2):
                        name = f"sc{k}"
                        pe.wait_ge(*freed(name, l, i))
                        for q in range(2):
                            last = mm(bank(name)[:, q * S:(q + 1) * S], Y[:, (2 * k + q) * P:(2 * k + q + 1) * P], Sw)
                        last.then_inc(*made(name))
                wait_alone(pe, *after("flags", l))
                runs, due = sweep_due(pe)
                with pe.If(due > 0):
                    for name in [f"sc{k}" for k in range(KT // 2)] + ["ht0", "ht1"]:
                        pe.wait_ge(*copied(name, l, NE // 2 - 1))
                    pe.wait_ge(sweep_dve, runs * SWEEP_DVE + 1)
                    for t in range(NT):
                        last = mm(ps[0:NE, 0, t * P:(t + 1) * P], comb2[:, t, :], ident)
                    last.then_inc(sweep_pe, 1)
                    pe.wait_ge(sweep_dve, runs * SWEEP_DVE + 2)
                    for e in range(NE):
                        last = mm(ps[:, e // 2, e % 2 * S:(e % 2 + 1) * S], K[0:NE, e:e + 1].to_broadcast([NE, P]), combT)
                    last.then_inc(sweep_pe, 1)
                    wait_alone(pe, sweep_dve, runs * SWEEP_DVE + 3)
                    with pe.Fori(0, NE) as e:
                        pe.wait_ge(sweep_load, runs * (NE * 96) + 96 + e * 96)
                        pe.wait_ge(sweep_dve, runs * SWEEP_DVE + 3 + e * 2)
                        for n in range(4):
                            w = ring[:, n, :].rearrange("p (k c) -> p k c", k=KT)
                            for q in range(2):
                                for k in range(KT):
                                    last = mm(ps[:, n, q * S:(q + 1) * S], w[:, k, q * P:(q + 1) * P], XN[:, k, :], k == 0, k == KT - 1)
                        last.then_inc(sweep_pe, 1)
                        pe.wait_ge(sweep_dve, runs * SWEEP_DVE + 4 + e * 2)
                        for half in range(2):
                            w = ring[:, 4 + half, :].rearrange("p (k c) -> p k c", k=4)
                            for q in range(KT // 2):
                                o = ps[:, (4 + q // 2) if half == 0 else q // 2, q % 2 * S:(q % 2 + 1) * S]
                                for k in range(4):
                                    last = mm(o, w[:, k, q * P:(q + 1) * P], hT[:, k, :], k == 0, k == 3)
                            last.then_inc(sweep_pe, 1)
                    wait_alone(pe, sweep_dve, runs * SWEEP_DVE + SWEEP_DVE)
            pe.wait_ge(*copied("sc7", DEPTH - 1, NE // 2 - 1))
            for t in range(NT):
                for g in range(KT // 4):
                    name = f"f{t * KT // 4 + g}"
                    pe.wait_ge(*freed(name))
                    for q in range(4):
                        last = pe.transpose(bank(name)[:, q * P:(q + 1) * P], X[:, 4 * g + q, t * P:(t + 1) * P], ident)
                    last.then_inc(*made(name))

        def pcol(r):
            return col[:, r:r + 1]

        def pcol96(r):
            return col96[:, r:r + 1]

        def t_h(ap, h):
            return ap.rearrange("p t (h w) -> p t h w", h=h)

        def main_dst(name, i=0):
            j = int(name[1:]) + NSLOT * (MAIN_ITERS - 1 if name[0] == "z" else i)
            return DQ + j * CH

        qv, kv = t_h(q_mla, H_A), t_h(k_mla, H_A)
        MAGIC = 12582912.0
        PI = float(np.pi)
        C1 = 6.28125
        C2 = float(np.round((2 * np.pi - C1) * 2 ** 20) / 2 ** 20)
        C3 = float(2 * np.pi - C1 - C2)

        @block.vector
        def _(dve):
            own = Steps(dve, dve_steps, DVE_PRE, DVE_LAYER)

            def do(ins):
                own.did(ins)
                own.wait()

            dve.memset(ones[:, :], 1.0).then_inc(ones_set, 1)
            dve.memset(eps[:, :], EPS).then_inc(ones_set, 1)
            own.did(dve.memset(fl[:, :], 0.0))
            for j in range(0, NT * KT // 4, 2):
                t, g = j // (KT // 4), j % (KT // 4)
                dve.wait_ge(*ready(f"x{j}"))
                dve.tensor_copy(X[:, 4 * g:4 * g + 4, t * P:(t + 1) * P],
                                bank(f"x{j}").rearrange("p (k s) -> p k s", k=4)).then_inc(*read(f"x{j}"))
            for l in range(DEPTH):
                dve.wait_ge(*ready(f"par{l}"))
                dve.tensor_copy(par[:, l, :], bank(f"par{l}")[:, 0:N_ROW]).then_inc(*read(f"par{l}"))
                dve.wait_ge(*ready(f"par96{l}"))
                dve.tensor_copy(par96[:, l, :], bank(f"par96{l}")[0:CB, 0:N_ROW96]).then_inc(*read(f"par96{l}"))
            dve.wait_ge(bias_in, 48)
            dve.wait_ge(*ready("bias"))
            dve.tensor_tensor(fbias, bank("bias")[0:H_D, :], lnc, ALU.add).then_inc(*read("bias"))
            dve.wait_ge(pos_in, 16)
            dve.wait_ge(const_in, 16)
            do(dve.tensor_copy(pos_f[:, :], pos_i[:, :]))
            for t in range(NT):
                own.did(dve.tensor_scalar(ang[:, 0, t, :], K[:, K_FREQ:K_FREQ + HALF], pos_f[:, t:t + 1], None, ALU.mult))
            own.wait()
            for n, turn in enumerate((0.25, 0.0)):
                k, r = ang[:, 1, :, :], ang[:, 2 + n, :, :]
                do(dve.tensor_scalar(k, ang[:, 0, :, :], 1.0 / (2 * PI), turn, ALU.mult, ALU.add))
                do(dve.tensor_scalar(k, k, MAGIC, None, ALU.add))
                do(dve.tensor_scalar(k, k, -MAGIC, None, ALU.add))
                do(dve.scalar_tensor_tensor(r, k, -C1, ang[:, 0, :, :], ALU.mult, ALU.add))
                do(dve.scalar_tensor_tensor(r, k, -C2, r, ALU.mult, ALU.add))
                do(dve.scalar_tensor_tensor(r, k, -C3, r, ALU.mult, ALU.add))
                do(dve.tensor_scalar(r, r, turn * 2 * PI, PI, ALU.add, ALU.min))
                ins = dve.tensor_scalar(r, r, -PI, None, ALU.max)
                ins.then_inc(ang_set, 1)
            for j in range(1, NT * KT // 4, 2):
                dve.wait_ge(*copied(f"x{j}"))
            for j in range(0, NT * KT // 4, 2):
                dve.wait_ge(*copied(f"x{j}"))
            dve.wait_ge(*copied(f"par96{DEPTH - 1}"))
            wait_parameters(dve)

            def keep(name, l, lo, w, i=0):
                dve.wait_ge(*ready(name, l, i))
                for t in range(NT):
                    ins = dve.tensor_scalar(PR[:, t, lo:lo + w], bank(name)[:, t * CH:t * CH + w], rstd_x[:, t:t + 1], None, ALU.mult)
                ins.then_inc(*read(name))

            def max_of(name, l, b, scale):
                dve.wait_ge(*ready(name, l))
                do(dve.tensor_reduce(mx[:, b, :], bank(name).rearrange("p (t n) -> p t n", t=NT), AX, ALU.max))
                dve.tensor_scalar(nmx[:, b, :], mx[:, b, :], -scale, None, ALU.mult).then_inc(*signal("nmax"))

            def convolve(m, taps, l):
                if taps[0] == TAPS // 2:
                    dve.wait_ge(*copied(f"mu{m}", l))
                for j in taps:
                    s = j - TAPS // 2
                    lo, hi = max(0, -s), S - max(0, s)
                    if s:
                        own.wait()
                    for c in (2 * m, 2 * m + 1):
                        if s == 0:
                            ins = dve.tensor_scalar(uc[:, c, :], u_raw[:, c, :], pcol96(R_CW + j * NCB + c), pcol96(R_CB + c), ALU.mult, ALU.add)
                        else:
                            ins = dve.scalar_tensor_tensor(uc[:, c, lo:hi], u_raw[:, c, lo + s:hi + s], pcol96(R_CW + j * NCB + c),
                                                           uc[:, c, lo:hi], ALU.mult, ALU.add)
                        if j == TAPS - 1 and c == 2 * m + 1:
                            ins.then_inc(*signal("conv"))
                        else:
                            own.did(ins)

            def attention(kind, n_heads, scale, l):
                for s in range(1, n_heads + 2):
                    if s <= n_heads:
                        max_of(f"{kind}s{s - 1}", l, (s - 1) % 2, scale)
                    if s >= 2:
                        h = s - 2
                        dve.wait_ge(*copied(f"{kind}s{h}", l))
                        dve.reciprocal(rs[:, h % 4, :], psum_p[:, h % 2, :]).then_inc(*signal("rsum"))
                        dve.wait_ge(*ready(f"{kind}p{h}", l))
                        dve.tensor_copy(pT[:, h % 2, :, :].rearrange("p t n -> p (t n)"), bank(f"{kind}p{h}")).then_inc(*read(f"{kind}p{h}"))
                    if kind == "d" and s <= 3 * (NCB // 2):
                        convolve((s - 1) // 3, ((2, 0), (1, 3), (4,))[(s - 1) % 3], l)

            with dve.Fori(0, DEPTH) as l:
                own.enter_layer(l)

                def bias_row(lo, n):
                    return brow[:, bass.ds(l, 1), lo:lo + n].to_broadcast([P, NT, n])

                dve.wait_ge(psum_free[SCATTER_BANKS[-1]], BANKS.count["pre"][SCATTER_BANKS[-1]] + l * BANKS.count["layer"][SCATTER_BANKS[-1]])
                dve.tensor_scalar(col[:, :].unsqueeze(1), par[:, bass.ds(l, 1), :], 1.0, None, ALU.mult).then_inc(*signal("cols"))
                dve.tensor_scalar(col96[:, :].unsqueeze(1), par96[:, bass.ds(l, 1), :], 1.0, None, ALU.mult).then_inc(*signal("cols"))
                dve.wait_ge(*after("cols", l, 1))
                for k in range(KT):
                    dve.tensor_scalar(XN[:, k, :], X[:, k, :], pcol(R_MIX + k), None, ALU.mult).then_inc(*signal("xg"))
                dve.wait_ge(*copied("ssq", l))
                dve.reciprocal(rstd_x[:, :], std_x[:, :]).then_inc(*signal("rstd_x"))
                dve.wait_ge(*after("rstd_x", l))
                keep("c1", l, CH, CH)
                keep("c2", l, 2 * CH, 48)
                dve.wait_ge(*after("lat_std", l))
                do(dve.reciprocal(rstd_lat[:, :, :], std_lat[:, :, :]))
                for t in range(NT):
                    for n, (lo, w) in enumerate(((CQ, QR), (CKV, KVR))):
                        ins = dve.tensor_scalar(PR[:, t, lo:lo + w], PR[:, t, lo:lo + w], rstd_lat[:, n, t:t + 1], None, ALU.mult)
                        if t < NT - 1 or n == 0:
                            own.did(ins)
                        else:
                            ins.then_inc(*signal("lat_n"))
                for t in range(NT):
                    dve.wait_ge(*ready(f"lat{t}", l))
                    for k in range(4):
                        ins = dve.tensor_scalar(latT[:, k, t * P:(t + 1) * P], bank(f"lat{t}")[:, k * P:(k + 1) * P], pcol(R_CQ + k), None, ALU.mult)
                    ins.then_inc(*read(f"lat{t}"))
                dve.wait_ge(*copied("c2", l))
                dve.tensor_tensor(PR[:, :, MG:MG + 16], PR[:, :, MG:MG + 16], bias_row(0, 16), ALU.add).then_inc(*signal("gate_b"))
                dve.wait_ge(ang_set, 2 + 1)
                kr1, kr2 = PR[:, :, KR:KR + HALF], PR[:, :, KR + HALF:KR + ROPE]
                for n, (x, c) in enumerate(((kr1, 0), (kr2, 1), (kr1, 1), (kr2, 0))):
                    own.did(dve.tensor_tensor(rt[:, n, :, :], x, cs[:, c, :, :], ALU.mult))
                own.wait()
                own.did(dve.tensor_tensor(rt[:, 4, :, :], rt[:, 0, :, :], rt[:, 1, :, :], ALU.subtract))
                do(dve.tensor_tensor(rt[:, 5, :, :], rt[:, 2, :, :], rt[:, 3, :, :], ALU.add))
                for n in range(2):
                    own.did(dve.tensor_copy(kv[:, :, :, NOPE + n * HALF:NOPE + (n + 1) * HALF],
                                            rt[:, 4 + n, :, :].unsqueeze(2).to_broadcast([P, NT, H_A, HALF])))
                for t in range(NT):
                    for j in (2, 3):
                        name = f"up{t}{j}"
                        h = 4 * (j - 2)
                        src = bank(name).rearrange("p (h w) -> p h w", h=4)
                        dve.wait_ge(*ready(name, l))
                        dve.tensor_copy(kv[:, t, h:h + 4, 0:NOPE], src[:, :, 0:NOPE])
                        dve.tensor_copy(v_mla[:, t, h * DV_A:(h + 4) * DV_A].rearrange("p (h w) -> p h w", h=4),
                                        src[:, :, NOPE:]).then_inc(*read(name))
                dve.wait_ge(*copied("up01", l))
                dve.wait_ge(*copied("up11", l))
                own.wait()
                x1, x2 = qv[:, :, :, NOPE:NOPE + HALF], qv[:, :, :, NOPE + HALF:]
                cos, sin = (cs[:, n, :, :].unsqueeze(2).to_broadcast([P, NT, H_A, HALF]) for n in range(2))
                for n, (x, c) in enumerate(((x1, cos), (x2, sin), (x1, sin), (x2, cos))):
                    own.did(dve.tensor_tensor(rtmp[:, n, :, :, :], x, c, ALU.mult))
                own.wait()
                own.did(dve.tensor_tensor(x1, rtmp[:, 0, :, :, :], rtmp[:, 1, :, :, :], ALU.subtract))
                dve.tensor_tensor(x2, rtmp[:, 2, :, :, :], rtmp[:, 3, :, :, :], ALU.add).then_inc(*signal("a_roped"))
                dve.wait_ge(*after("a_sq", l))
                own.did(dve.tensor_reduce(ss_a[:, 0, :, :], t_h(PR[:, :, DV:DV + W_D], H_A), AX, ALU.add))
                dve.tensor_reduce(ss_a[:, 1, :, :], t_h(PR[:, :, MU:MU + W_M], H_A), AX, ALU.add).then_inc(*signal("a_ss"))
                dve.wait_ge(*after("a_std", l))
                do(dve.reciprocal(rstd_a[:, :, :, :], std_a[:, :, :, :]))
                own.did(dve.tensor_tensor(qv, qv, rstd_a[:, 0, :, :].unsqueeze(3).to_broadcast([P, NT, H_A, QK_A]), ALU.mult))
                dve.tensor_tensor(kv, kv, rstd_a[:, 1, :, :].unsqueeze(3).to_broadcast([P, NT, H_A, QK_A]), ALU.mult).then_inc(*signal("a_n"))
                for j in range(1, NSLOT, 2):
                    keep(f"m{j}", l, main_dst(f"m{j}", 0), CH, 0)
                dve.wait_ge(*after("d_sq", l))
                own.did(dve.tensor_reduce(ss_d[:, 0, :, :], t_h(PR[:, :, DV:DV + W_D], H_D), AX, ALU.add))
                dve.tensor_reduce(ss_d[:, 1, :, :], t_h(PR[:, :, MU:MU + W_M], H_D), AX, ALU.add).then_inc(*signal("d_ss"))
                dve.wait_ge(*after("d_std", l))
                do(dve.reciprocal(rstd_d[:, :, :, :], std_d[:, :, :, :]))
                do(dve.tensor_scalar(rstd_d[:, 0, :, :], rstd_d[:, 0, :, :], HD_D ** -0.5, None, ALU.mult))
                for n, lo in enumerate((DQ, DK)):
                    w = t_h(PR[:, :, lo:lo + W_D], H_D)
                    ins = dve.tensor_tensor(w, w, rstd_d[:, n, :, :].unsqueeze(3).to_broadcast([P, NT, H_D, HD_D]), ALU.mult)
                    if n == 0:
                        own.did(ins)
                    else:
                        ins.then_inc(*signal("d_n"))
                for j in range(1, NSLOT, 2):
                    keep(f"m{j}", l, main_dst(f"m{j}", 1), CH, 1)
                attention("a", H_A, QK_A ** -0.5, l)
                for j in range(1, NSLOT, 2):
                    keep(f"z{j}", l, main_dst(f"z{j}"), CH)
                attention("d", H_D, 1.0, l)

                for d in range(2):
                    name = f"rows{d}"
                    g_i, g_f = bank(name)[0:H_M, 0:S], bank(name)[0:H_M, S:2 * S]

                    def way(r):
                        return r if d == 0 else r[:, ::-1]

                    dve.wait_ge(*ready(name, l))
                    dve.wait_ge(*after("gate_ln", l, d))
                    do(dve.scalar_tensor_tensor(grow(d, 3), g_f, 0.0, grow(d, 0), ALU.min, ALU.subtract))
                    do(dve.tensor_tensor_scan(way(grow(d, 1)), ones[0:H_M, 0:1].to_broadcast([H_M, S]), way(grow(d, 3)), 0.0, ALU.mult, ALU.add))
                    dve.tensor_tensor(grow(d, 2), g_i, grow(d, 1), ALU.subtract).then_inc(*read(name))
                    dve.wait_ge(*copied(name, l))
                    do(dve.tensor_tensor_scan(way(grow(d, 3)), way(grow(d, 2)), way(grow(d, 2)), 0.0, ALU.max, ALU.max))
                    own.did(dve.tensor_scalar(grow(d, 0), grow(d, 3), -1.0, None, ALU.mult))
                    dve.scalar_tensor_tensor(grow(d, 4), grow(d, 1), -1.0, grow(d, 3), ALU.mult, ALU.subtract).then_inc(*signal("rows_ready"))
                dve.wait_ge(*ready("gcols", l))
                dve.tensor_copy(gcol[:, :, :, :, :].rearrange("p n d t h -> p (n d t h)"), bank("gcols")[:, 0:32]).then_inc(*read("gcols"))
                for h in range(H_M + 1):
                    if h < H_M:
                        dve.wait_ge(*ready(f"mk{h}", l))
                        dve.tensor_scalar(mqk[:, h % 2, 1, :], bank(f"mk{h}")[0:CB, :], HD_M ** -0.5, None, ALU.mult).then_inc(*read(f"mk{h}"))
                        dve.wait_ge(*ready(f"ms{h}", l))
                        dve.wait_ge(*copied(f"w{h}0", l))
                        dve.wait_ge(*copied(f"w{h}1", l))
                        for d, lo, hi, src in ((0, 0, S, 0), (0, S, S + P, S + P), (1, 0, P, 0), (1, P, P + S, S)):
                            w = decay[:, h % 2, d, lo:hi]
                            ins = dve.tensor_tensor(w, w, bank(f"ms{h}")[:, src:src + hi - lo], ALU.mult)
                        ins.then_inc(*read(f"ms{h}"))
                    if h >= 1:
                        g = h - 1
                        dens = [bank(f"n{g}{d}").rearrange("p (t n) -> p t n", t=NT)[:, :, HD_M] for d in range(2)]
                        for d in range(2):
                            dve.wait_ge(*ready(f"n{g}{d}", l))
                            own.did(dve.tensor_scalar(dn[:, 1, d, :], dens[d], -1.0, None, ALU.mult))
                        own.wait()
                        for d in range(2):
                            own.did(dve.tensor_tensor(dn[:, 0, d, :], dn[:, 1, d, :], dens[d], ALU.max))
                        dve.wait_ge(*after("em_ready", l))
                        own.wait()
                        do(dve.tensor_tensor(dn[:, 0, :, :], dn[:, 0, :, :], em[:, :, :, g], ALU.max))
                        dve.reciprocal(dn[:, 1, :, :], dn[:, 0, :, :]).then_inc(*signal("r_ready"))
                        dve.wait_ge(*after("r_ready", l, g))
                        dve.wait_ge(*copied(f"n{g}0", l))
                        for t in range(NT):
                            h_row = PR[:, t, MU + g * HD_M:MU + (g + 1) * HD_M]
                            ins = dve.scalar_tensor_tensor(h_row, bank(f"n{g}1")[:, t * S:t * S + HD_M], dn[:, 1, 1, t:t + 1], h_row, ALU.mult, ALU.add)
                        ins.then_inc(*read(f"n{g}1"))
                dve.wait_ge(*after("m_std", l))
                do(dve.reciprocal(rstd_m[:, :, :], std_m[:, :, :]))
                for t in range(NT):
                    for h in range(H_M):
                        y, o = (PR[:, t, c + h * HD_M:c + (h + 1) * HD_M] for c in (MU, MO))
                        ins = dve.scalar_tensor_tensor(y, y, rstd_m[:, h, t:t + 1], o, ALU.mult, ALU.mult)
                        if t == NT - 1 and h == H_M - 1:
                            ins.then_inc(*signal("y_ml"))
                for j in range(1, KT // 2, 2):
                    dve.wait_ge(*ready(f"y{j}", l))
                    for q in range(2):
                        kk = 2 * j + q
                        src = bank(f"y{j}")[:, q * S:(q + 1) * S]
                        if kk < 10:
                            ins = dve.tensor_copy(XN[:, kk, :], src)
                        else:
                            ins = dve.tensor_scalar(XN[:, kk, :], src, pcol(R_MLO + kk - 10), None, ALU.mult)
                    ins.then_inc(*read(f"y{j}"))
                for j in range(N_OUT):
                    dve.wait_ge(*ready(f"o{j}", l))
                    x = X[:, 2 * j:2 * j + 2, :].rearrange("p k s -> p (k s)")
                    dve.tensor_tensor(x, x, bank(f"o{j}"), ALU.add).then_inc(*read(f"o{j}"))
                std2, rstd2 = scr[:, 1024:1280], scr[:, 1280:1536]
                dve.wait_ge(*copied("ssq2", l))
                do(dve.reciprocal(rstd2, std2))
                for k in range(KT):
                    dve.scalar_tensor_tensor(XN[:, k, :], X[:, k, :], pcol(R_FFN + k), rstd2, ALU.mult, ALU.mult).then_inc(*signal("xn2"))
                for t in range(NT):
                    dve.wait_ge(*ready(f"route{t}", l))
                    dve.tensor_tensor(lg[:, t:t + 1, :], bank(f"route{t}")[:, 0:NG + NE].unsqueeze(1),
                                      brow[:, bass.ds(l, 1), 16:16 + NG + NE], ALU.add).then_inc(*read(f"route{t}"))
                for t in range(NT):
                    dve.wait_ge(*copied(f"route{t}", l))
                own.did(dve.memset(routed, 0.0))
                own.did(dve.tensor_scalar(tri, mask, -1.0, None, ALU.is_ge))
                own.did(dve.tensor_tensor_scan(iota, ones[:, 0:CAP], ones[:, 0:CAP], -1.0, ALU.mult, ALU.add))
                g4, e16 = lg[:, :, 0:NG], lg[:, :, NG:]

                def over(ap, n):
                    return ap.unsqueeze(2).to_broadcast([P, NT, n])

                def key_row(lo, n):
                    return K[:, lo:lo + n].unsqueeze(1).to_broadcast([P, NT, n])

                def first_of(o, x, top, keys, n):
                    do(dve.tensor_tensor(o, x, over(top, n), ALU.is_equal))
                    do(dve.tensor_tensor(o, o, keys, ALU.mult))
                    do(dve.tensor_reduce(rs1[:, 3, :], o, AX, ALU.max))
                    do(dve.tensor_tensor(o, o, over(rs1[:, 3, :], n), ALU.is_equal))

                do(dve.tensor_reduce(rs1[:, 0, :], g4, AX, ALU.max))
                dve.tensor_tensor(rt[:, 0, :, 0:NG], g4, over(rs1[:, 0, :], NG), ALU.subtract).then_inc(*signal("e_in"))
                ohg = rt[:, 3, :, 0:NG]
                first_of(ohg, g4, rs1[:, 0, :], key_row(K_KEYG, NG), NG)
                do(dve.tensor_scalar(ohg, ohg, -1.0, -NEG, ALU.add, ALU.mult))
                dve.wait_ge(*after("e_exp", l, 0))
                do(dve.tensor_reduce(rs1[:, 1, :], rt[:, 1, :, 0:NG], AX, ALU.add))
                own.did(dve.reciprocal(rs1[:, 2, :], rs1[:, 1, :]))
                do(dve.tensor_tensor(rt[:, 4, :, :].rearrange("p t (g e) -> p t g e", g=NG), e16.rearrange("p t (g e) -> p t g e", g=NG),
                                     ohg.unsqueeze(3).to_broadcast([P, NT, NG, EPG]), ALU.add))
                do(dve.tensor_reduce(rs1[:, 4, :], rt[:, 4, :, :], AX, ALU.max))
                first_of(rt[:, 1, :, :], rt[:, 4, :, :], rs1[:, 4, :], key_row(K_KEYE, NE), NE)
                do(dve.scalar_tensor_tensor(rt[:, 4, :, :], rt[:, 1, :, :], 2 * NEG, rt[:, 4, :, :], ALU.mult, ALU.add))
                do(dve.tensor_reduce(rs1[:, 5, :], rt[:, 4, :, :], AX, ALU.max))
                dve.tensor_tensor(rs1[:, 6, :], rs1[:, 5, :], rs1[:, 4, :], ALU.subtract).then_inc(*signal("e_in"))
                first_of(rt[:, 2, :, :], rt[:, 4, :, :], rs1[:, 5, :], key_row(K_KEYE, NE), NE)
                dve.tensor_tensor(picked[:, :, 0:NE], rt[:, 1, :, :], rt[:, 2, :, :], ALU.add).then_inc(*signal("picked"))
                dve.wait_ge(*after("e_exp", l, 1))
                do(dve.tensor_scalar(rs1[:, 3, :], rs1[:, 7, :], 1.0, None, ALU.add))
                do(dve.reciprocal(rs1[:, 0, :], rs1[:, 3, :]))
                do(dve.tensor_tensor(rs1[:, 0, :], rs1[:, 0, :], rs1[:, 2, :], ALU.mult))
                do(dve.tensor_tensor(rs1[:, 1, :], rs1[:, 0, :], rs1[:, 7, :], ALU.mult))
                own.did(dve.tensor_tensor(rt[:, 1, :, :], rt[:, 1, :, :], over(rs1[:, 0, :], NE), ALU.mult))
                do(dve.tensor_tensor(rt[:, 2, :, :], rt[:, 2, :, :], over(rs1[:, 1, :], NE), ALU.mult))
                do(dve.tensor_tensor(comb[:, :, 0:NE], rt[:, 1, :, :], rt[:, 2, :, :], ALU.add))
                dve.wait_ge(*ready("rank", l))
                own.did(dve.tensor_reduce(rs1[:, 4, 0:1], bank("rank")[:, 2 * NE:3 * NE], AX, ALU.max))
                dve.tensor_tensor(rank[:, :, 0:NE], bank("rank")[:, 0:2 * NE].rearrange("p (t e) -> p t e", t=NT), picked[:, :, 0:NE],
                                  ALU.subtract).then_inc(*read("rank"))
                do(dve.tensor_tensor(fl[:, 1:2], fl[:, 1:2], fl[:, 0:1], ALU.add))
                do(dve.tensor_scalar(fl[:, 0:1], rs1[:, 4, 0:1], float(CAP), None, ALU.is_gt))
                dve.tensor_copy(fi[:, :], fl[:, :]).then_inc(*signal("flags"))
                dve.wait_ge(*copied("rank", l))

                def one_hot(o, e, w):
                    for t in range(NT):
                        ins = dve.tensor_scalar(o[:, t, :], iota, rank[:, t, e], w[:, t, e], ALU.is_equal, ALU.mult)
                    return ins

                def tokens_of_pair(i):
                    for j in range(2):
                        ins = one_hot(Gm[:, :, j * CAP:(j + 1) * CAP], bass.ds(2 * i + j, 1), picked)
                    ins.then_inc(*signal("gm"))

                tokens_of_pair(0)
                with dve.Fori(0, NE // 2) as i:
                    for half in range(2):
                        dve.wait_ge(*copied(f"g{half}", l, i))
                        dve.wait_ge(*ready(f"u{half}", l, i))
                        dve.tensor_tensor(gated[:, half * CH:(half + 1) * CH], sgs[:, half * CH:(half + 1) * CH],
                                          bank(f"u{half}")[0:2 * CAP, 0:CH], ALU.mult).then_inc(*read(f"u{half}"))
                        if half == 0:
                            tokens_of_pair(i + 1)
                            for j in range(2):
                                ins = one_hot(Gw[:, :, j * CAP:(j + 1) * CAP], bass.ds(2 * i + j, 1), comb)
                            ins.then_inc(*signal("gw"))
                        else:
                            dve.wait_ge(*ready("sw", l, i))
                            dve.tensor_copy(Sw, bank("sw")[0:2 * CAP, 0:S]).then_inc(*read("sw"))
                        dve.wait_ge(*ready(f"ht{half}", l, i))
                        dve.tensor_copy(hs[:, 2 * half:2 * half + 2, :].rearrange("p k n -> p (k n)"), bank(f"ht{half}")[:, 0:4 * CAP]).then_inc(*read(f"ht{half}"))
                    for n in (1, 3):
                        dve.wait_ge(*ready(f"dy{n}", l, i))
                        dve.tensor_copy(Y[:, n * 512:(n + 1) * 512], bank(f"dy{n}")[0:2 * CAP, :]).then_inc(*read(f"dy{n}"))
                    for k in range(KT // 2):
                        name = f"sc{k}"
                        dve.wait_ge(*ready(name, l, i))
                        x = X[:, 2 * k:2 * k + 2, :].rearrange("p k s -> p (k s)")
                        dve.tensor_tensor(x, x, bank(name), ALU.add).then_inc(*read(name))
                runs, due = sweep_due(dve)
                with dve.If(due > 0):
                    dve.scalar_tensor_tensor(comb2, rank[:, :, 0:NE], CAP - 0.5, comb[:, :, 0:NE], ALU.is_gt, ALU.mult).then_inc(sweep_dve, 1)
                    dve.wait_ge(sweep_pe, runs * SWEEP_PE + 1)
                    dve.tensor_copy(combT, ps[0:NE, 0, 0:S]).then_inc(sweep_dve, 1)
                    dve.wait_ge(sweep_pe, runs * SWEEP_PE + 2)
                    dve.wait_ge(sweep_dve, runs * SWEEP_DVE + 1)
                    for b in range(8):
                        ins = dve.tensor_copy(combB[:, 2 * b:2 * b + 2, :].rearrange("p e s -> p (e s)"), ps[:, b, :])
                    ins.then_inc(sweep_dve, 1)
                    with dve.Fori(0, NE) as e:
                        dve.wait_ge(sweep_act, runs * NE + 1 + e)
                        for half in range(2):
                            ins = dve.tensor_tensor(hT[:, 2 * half:2 * half + 2, :].rearrange("p k n -> p (k n)"), sg[:, half, :],
                                                    ps[:, 2 * half + 1, :], ALU.mult)
                        ins.then_inc(sweep_own, 1)
                        dve.wait_ge(sweep_own, runs * NE + 1 + e)
                        dve.wait_ge(sweep_dve, runs * SWEEP_DVE + 3 + e * 2)
                        dve.tensor_tensor(hT, hT, combB[:, bass.ds(e, 1), :].to_broadcast([P, 4, S]), ALU.mult).then_inc(sweep_dve, 1)
                        for k in range(KT // 2):
                            dve.wait_ge(sweep_pe, runs * SWEEP_PE + (4 + k // 4) + e * 3)
                            x = X[:, 2 * k:2 * k + 2, :].rearrange("p k s -> p (k s)")
                            ins = dve.tensor_tensor(x, x, ps[:, (4 + k) % 8, :], ALU.add)
                        ins.then_inc(sweep_dve, 1)
                    wait_alone(dve, sweep_dve, runs * SWEEP_DVE + SWEEP_DVE)
                own.leave_layer()
            for j in range(0, NT * KT // 4, 2):
                t, g = j // (KT // 4), j % (KT // 4)
                dve.wait_ge(*ready(f"f{j}"))
                dve.tensor_copy(PR[:, t, g * 512:(g + 1) * 512], bank(f"f{j}")).then_inc(*read(f"f{j}"))

        @block.scalar
        def _(act):
            own = Steps(act, act_steps, 0, ACT_LAYER)
            for l in range(DEPTH):
                load_rows96(act, l, rows_in)
                load_biases(act, l, rows_in)

            def do(ins):
                own.did(ins)
                own.wait()

            for j in range(1, NT * KT // 4, 2):
                t, g = j // (KT // 4), j % (KT // 4)
                act.wait_ge(*ready(f"x{j}"))
                act.activation(X[:, 4 * g:4 * g + 4, t * P:(t + 1) * P],
                               bank(f"x{j}").rearrange("p (k s) -> p k s", k=4), ACT.Copy).then_inc(*read(f"x{j}"))
            act.wait_ge(ones_set, 2)
            for n in range(2):
                act.wait_ge(ang_set, n + 1)
                ins = act.activation(cs[:, n, :, :], ang[:, 2 + n, :, :], ACT.Sin)
            ins.then_inc(ang_set, 1)
            for j in range(NT * KT // 4):
                act.wait_ge(*copied(f"x{j}"))
            act.wait_ge(*copied(f"par96{DEPTH - 1}"))

            def keep(name, l, lo, w, i=0):
                act.wait_ge(*ready(name, l, i))
                for t in range(NT):
                    ins = act.activation(PR[:, t, lo:lo + w], bank(name)[:, t * CH:t * CH + w], ACT.Copy, scale=rstd_x[:, t:t + 1])
                ins.then_inc(*read(name))

            with act.Fori(0, DEPTH) as l:
                own.enter_layer(l)

                def attention(kind, n_heads, per, scale, n_first, cols, out_col, w):
                    for s in range(n_heads + 3):
                        if s < n_heads and s % per == 0:
                            name = f"{kind}t{s // per}"
                            act.wait_ge(*ready(name, l))
                            for n in range(2):
                                ins = act.activation(qkT[0:w, s // per % 2, n * S:(n + 1) * S], bank(name)[0:w, n * S:(n + 1) * S],
                                                     ACT.Copy, scale=cols[n])
                            ins.then_inc(*read(name))
                        if 1 <= s <= n_heads:
                            h = s - 1
                            act.wait_ge(*after("nmax", l, n_first + h))
                            for t in range(NT):
                                ins = act.activation(prob[:, h % 2, t, :], bank(f"{kind}s{h}")[:, t * S:(t + 1) * S], ACT.Exp,
                                                     bias=nmx[:, h % 2, t:t + 1], scale=scale, accum_out=psum_p[:, h % 2, t:t + 1])
                            ins.then_inc(*read(f"{kind}s{h}"))
                        if s >= 3:
                            h = s - 3
                            act.wait_ge(*after("rsum", l, n_first + h))
                            act.wait_ge(*ready(f"{kind}o{h}", l))
                            for t in range(NT):
                                ins = act.activation(PR[:, t, out_col + h * 64:out_col + (h + 1) * 64], bank(f"{kind}o{h}")[:, t * 64:(t + 1) * 64],
                                                     ACT.Copy, scale=rs[:, h % 4, t:t + 1])
                            ins.then_inc(*read(f"{kind}o{h}"))

                act.wait_ge(psum_free[SCATTER_BANKS[-1]], BANKS.count["pre"][SCATTER_BANKS[-1]] + l * BANKS.count["layer"][SCATTER_BANKS[-1]])
                for q in range(4):
                    act.activation(SQ[:, 4 * q:4 * q + 4, :].rearrange("p k s -> p (k s)"),
                                   X[:, 4 * q:4 * q + 4, :].rearrange("p k s -> p (k s)"), ACT.Square).then_inc(*signal("sq"))
                act.wait_ge(*ready("ssq", l))
                act.activation(std_x[:, :], bank("ssq")[:, 0:NT], ACT.Sqrt, bias=eps[:, 0:1], scale=1.0 / D).then_inc(*read("ssq"))
                act.wait_ge(*after("rstd_x", l))
                act.wait_ge(*after("cols", l, 1))
                keep("c0", l, 0, CH)
                act.wait_ge(*copied("c0", l))
                act.wait_ge(*copied("c1", l))
                for t in range(NT):
                    for n, (lo, w) in enumerate(((CQ, QR), (CKV, KVR))):
                        dump = scr[:, 1024 + t * 512 + lo:1024 + t * 512 + lo + w]
                        own.did(act.activation(dump, PR[:, t, lo:lo + w], ACT.Square, accum_out=ss_lat[:, n, t:t + 1]))
                own.wait()
                own.did(act.activation(std_lat[:, 0, :], ss_lat[:, 0, :], ACT.Sqrt, bias=eps[:, 0:1], scale=1.0 / QR))
                act.activation(std_lat[:, 1, :], ss_lat[:, 1, :], ACT.Sqrt, bias=eps[:, 0:1], scale=1.0 / KVR).then_inc(*signal("lat_std"))
                for t in range(NT):
                    for j in range(2):
                        name = f"up{t}{j}"
                        act.wait_ge(*ready(name, l))
                        act.activation(q_mla[:, t, j * 384:(j + 1) * 384], bank(name)[:, 0:384], ACT.Copy).then_inc(*read(name))
                act.wait_ge(*after("a_roped", l))
                own.did(act.activation(PR[:, :, DV:DV + W_D], q_mla, ACT.Square))
                act.activation(PR[:, :, MU:MU + W_M], k_mla, ACT.Square).then_inc(*signal("a_sq"))
                act.wait_ge(*after("a_ss", l))
                act.activation(std_a[:, :, :, :].rearrange("p n t h -> p (n t h)"), ss_a[:, :, :, :].rearrange("p n t h -> p (n t h)"), ACT.Sqrt, bias=eps[:, 0:1], scale=1.0 / QK_A).then_inc(*signal("a_std"))
                for j in range(0, NSLOT, 2):
                    keep(f"m{j}", l, main_dst(f"m{j}", 0), CH, 0)
                for j in range(NSLOT):
                    act.wait_ge(*copied(f"m{j}", l, 0))
                own.did(act.activation(PR[:, :, DV:DV + W_D], PR[:, :, DQ:DQ + W_D], ACT.Square))
                act.activation(PR[:, :, MU:MU + W_M], PR[:, :, DK:DK + W_D], ACT.Square).then_inc(*signal("d_sq"))
                act.wait_ge(*after("d_ss", l))
                act.activation(std_d[:, :, :, :].rearrange("p n t h -> p (n t h)"), ss_d[:, :, :, :].rearrange("p n t h -> p (n t h)"), ACT.Sqrt, bias=eps[:, 0:1], scale=1.0 / HD_D).then_inc(*signal("d_std"))
                for j in range(0, NSLOT, 2):
                    keep(f"m{j}", l, main_dst(f"m{j}", 1), CH, 1)
                act.wait_ge(bias_out, 16)
                attention("a", H_A, 1, QK_A ** -0.5, 0, (pcol96(R_AQ), pcol96(R_AK)), 0, QK_A)
                for j in range(0, NSLOT, 2):
                    keep(f"z{j}", l, main_dst(f"z{j}"), CH)
                for m in range(NCB // 2):
                    act.wait_ge(*ready(f"mu{m}", l))
                    act.activation(u_raw[:, 2 * m:2 * m + 2, :].rearrange("p b s -> p (b s)"), bank(f"mu{m}")[0:CB, :], ACT.Copy).then_inc(*read(f"mu{m}"))
                attention("d", H_D, 2, 1.0, H_A, (pcol(R_DQ), pcol(R_DK)), DQ, P)

                for d in range(2):
                    act.wait_ge(*ready(f"rows{d}", l))
                    do(act.activation(grow(d, 0), bank(f"rows{d}")[0:H_M, S:2 * S], ACT.Abs))
                    do(act.activation(grow(d, 0), grow(d, 0), ACT.Exp, scale=-1.0))
                    act.activation(grow(d, 0), grow(d, 0), ACT.Ln, bias=1.0).then_inc(*signal("gate_ln"))
                act.wait_ge(*copied("gcols", l))
                act.activation(em[:, :, :, :].rearrange("p d t h -> p (d t h)"), gcol[:, 1, :, :, :].rearrange("p d t h -> p (d t h)"),
                               ACT.Exp).then_inc(*signal("em_ready"))
                for h in range(H_M):
                    act.wait_ge(*after("conv", l, h))
                    u = uc[:, 2 * h:2 * h + 2, :].rearrange("p b s -> p (b s)")
                    act.activation(u, u, ACT.Silu).then_inc(*signal("uc_ready"))
                for h in range(H_M + 1):
                    if h < H_M:
                        act.wait_ge(*ready(f"mq{h}", l))
                        act.activation(mqk[:, h % 2, 0, :], bank(f"mq{h}")[0:CB, :], ACT.Copy).then_inc(*read(f"mq{h}"))
                        for d, cuts in ((0, ((0, S, 0), (S, S + P, 1))), (1, ((0, P, 0), (P, P + S, 1)))):
                            act.wait_ge(*ready(f"w{h}{d}", l))
                            for lo, hi, s in cuts:
                                ins = act.activation(decay[:, h % 2, d, lo:hi], bank(f"w{h}{d}")[:, lo:hi], ACT.Exp, bias=gcol[:, 0, d, s, h:h + 1])
                            ins.then_inc(*read(f"w{h}{d}"))
                    if h >= 1:
                        g = h - 1
                        act.wait_ge(*after("r_ready", l, g))
                        for t in range(NT):
                            ins = act.activation(PR[:, t, MU + g * HD_M:MU + (g + 1) * HD_M], bank(f"n{g}0")[:, t * S:t * S + HD_M],
                                                 ACT.Copy, scale=dn[:, 1, 0, t:t + 1])
                        ins.then_inc(*read(f"n{g}0"))
                        act.wait_ge(*copied(f"n{g}1", l))
                        if g:
                            own.wait()
                        for t in range(NT):
                            own.did(act.activation(scr[:, 2048 + t * HD_M:2048 + (t + 1) * HD_M], PR[:, t, MU + g * HD_M:MU + (g + 1) * HD_M], ACT.Square,
                                                   accum_out=ss_m[:, g, t:t + 1]))
                own.wait()
                own.did(act.activation(std_m[:, :, :].rearrange("p h t -> p (h t)"), ss_m[:, :, :].rearrange("p h t -> p (h t)"), ACT.Sqrt, bias=eps[:, 0:1], scale=1.0 / HD_M))
                act.activation(PR[:, :, MO:MO + W_M], PR[:, :, MO:MO + W_M], ACT.Sigmoid).then_inc(*signal("m_std"))
                for j in range(0, KT // 2, 2):
                    act.wait_ge(*ready(f"y{j}", l))
                    for q in range(2):
                        kk = 2 * j + q
                        src = bank(f"y{j}")[:, q * S:(q + 1) * S]
                        if kk < 10:
                            ins = act.activation(XN[:, kk, :], src, ACT.Copy)
                        else:
                            ins = act.activation(XN[:, kk, :], src, ACT.Copy, scale=pcol(R_MLO + kk - 10))
                    ins.then_inc(*read(f"y{j}"))
                for q in range(4):
                    act.wait_ge(*copied(f"o{2 * q}", l))
                    act.wait_ge(*copied(f"o{2 * q + 1}", l))
                    act.activation(SQ[:, 4 * q:4 * q + 4, :].rearrange("p k s -> p (k s)"),
                                   X[:, 4 * q:4 * q + 4, :].rearrange("p k s -> p (k s)"), ACT.Square).then_inc(*signal("sq2"))
                act.wait_ge(*ready("ssq2", l))
                act.activation(scr[:, 1024:1280], bank("ssq2")[:, 0:S], ACT.Sqrt, bias=eps[:, 0:1], scale=1.0 / D).then_inc(*read("ssq2"))
                def by_token(tiles):
                    for j in tiles:
                        act.wait_ge(*ready(f"xt{j}", l))
                        act.activation(xtok[:, j // (KT // 4), j % (KT // 4) * 512:(j % (KT // 4) + 1) * 512], bank(f"xt{j}"), ACT.Copy).then_inc(*read(f"xt{j}"))

                act.wait_ge(*after("e_in", l, 0))
                act.activation(rt[:, 1, :, 0:NG], rt[:, 0, :, 0:NG], ACT.Exp).then_inc(*signal("e_exp"))
                by_token(range(NT * KT // 8))
                act.wait_ge(*after("e_in", l, 1))
                act.activation(rs1[:, 7, :], rs1[:, 6, :], ACT.Exp).then_inc(*signal("e_exp"))
                by_token(range(NT * KT // 8, NT * KT // 4))

                def gathered(kind, i=0):
                    for n in range(4):
                        act.wait_ge(*ready(f"{kind}{n}", l, i))
                        act.activation(XG[:, 4 * n:4 * n + 4, :].rearrange("p k n -> p (k n)"),
                                       bank(f"{kind}{n}")[:, 0:8 * CAP], ACT.Copy).then_inc(*read(f"{kind}{n}"))

                gathered("gp")
                with act.Fori(0, NE // 2) as i:
                    for half in range(2):
                        act.wait_ge(*ready(f"g{half}", l, i))
                        act.activation(sgs[:, half * CH:(half + 1) * CH], bank(f"g{half}")[0:2 * CAP, 0:CH], ACT.Silu).then_inc(*read(f"g{half}"))
                    act.wait_ge(*ready("u1", l, i))
                    gathered("gx", i)
                    for n in (0, 2):
                        act.wait_ge(*ready(f"dy{n}", l, i))
                        act.activation(Y[:, n * 512:(n + 1) * 512], bank(f"dy{n}")[0:2 * CAP, :], ACT.Copy).then_inc(*read(f"dy{n}"))
                wait_alone(act, *after("flags", l))
                runs, due = sweep_due(act)
                with act.If(due > 0):
                    with act.Fori(0, NE) as e:
                        act.wait_ge(sweep_pe, runs * SWEEP_PE + 3 + e * 3)
                        for half in range(2):
                            ins = act.activation(sg[:, half, :], ps[:, 2 * half, :], ACT.Silu)
                        ins.then_inc(sweep_act, 1)
                    wait_alone(act, sweep_dve, runs * SWEEP_DVE + SWEEP_DVE)
                own.leave_layer()
            for j in range(1, NT * KT // 4, 2):
                t, g = j // (KT // 4), j % (KT // 4)
                act.wait_ge(*ready(f"f{j}"))
                act.activation(PR[:, t, g * 512:(g + 1) * 512], bank(f"f{j}"), ACT.Copy).then_inc(*read(f"f{j}"))



INPUTS = ["x", "positions", "rel_bias", "norm_mix", "w_in", "mla_norm_cq", "mla_w_uq", "mla_norm_ckv", "mla_w_ukv",
          "mla_q_norm", "mla_k_norm", "dil_q_norm", "dil_k_norm", "ml_conv_w", "ml_conv_b", "ml_w_q", "ml_w_k",
          "ml_gate_bias", "ml_out_norm", "w_out", "norm_ffn", "router_group_w", "router_group_b",
          "router_expert_w", "router_expert_b", "moe_w_gate", "moe_w_up", "moe_w_down"]


def kernel(**inputs):
    import concourse.bacc as bacc
    from concourse.bass_utils import run_bass_kernel_spmd

    nc = bacc.Bacc("TRN2", target_bir_lowering=False, num_devices=1)
    arrays, aps = {}, {}
    consts = dict(zip(("consts", "onehot", "lncount"), shape_constants()))
    for name, value in [(n, inputs[n]) for n in INPUTS] + list(consts.items()):
        v = np.ascontiguousarray(value)
        arrays[f"in_{name}"] = v
        aps[name] = nc.dram_tensor(f"in_{name}", v.shape, mybir.dt.from_np(v.dtype), kind="ExternalInput").ap()
    out = nc.dram_tensor("out", (1, S, D), F32, kind="ExternalOutput").ap()
    build(nc, aps, aps["consts"], aps["onehot"], aps["lncount"], out)
    return run_bass_kernel_spmd(nc, [arrays], core_ids=[0]).results[0]["out"]
```
